# Optimizing a Trainium2 kernel written in Bass

```python
import math
import jax, jax.numpy as jnp
from jax import lax
import numpy as np

D_MODEL = 1024
BATCH = 1
SEQ = 512
DEPTH = 2

GRID_W = 64
CTX_LEN = 256
NORM_EPS = 1e-6
NA_HEADS = 8
NA_HEAD_DIM = 64
NA_WIDTH = NA_HEADS * NA_HEAD_DIM
NA_MAX_ROWS = 8
NA_COLS = 16
HY_WIDTH = D_MODEL - NA_WIDTH
HY_ORDER = 2
HY_SHORT = 3
HY_EMB = 33
HY_BANDS = (HY_EMB - 1) // 2
HY_FFN = 64
HY_MIN_DECAY = math.log(1e-2) / 1.5
HY_MAX_DECAY = math.log(1e-2) / 0.3
EVEN_IN = 3 * NA_WIDTH + (HY_ORDER + 1) * HY_WIDTH
RW_HEAD = 64
RW_HEADS = D_MODEL // RW_HEAD
RW_DECAY_LORA = 64
RW_AAA_LORA = 64
RW_GATE_LORA = 160
RW_GN_EPS = 64e-5
FFN_HIDDEN = -(-8 * D_MODEL // (3 * 256)) * 256
N_EVEN = (DEPTH + 1) // 2
N_ODD = DEPTH // 2

kernel_name = 'hybrid_natten_hyena_rwkv7_dit'

def rms_norm(x, g):
    xf = x.astype(jnp.float32)
    y = xf * lax.rsqrt(jnp.mean(jnp.square(xf), axis=-1, keepdims=True) + NORM_EPS)
    return (y * g.astype(jnp.float32)).astype(x.dtype)

def shift_prev(x):
    return jnp.pad(x[:, :-1], ((0, 0), (1, 0), (0, 0)))

def shift_next(x):
    return jnp.pad(x[:, 1:], ((0, 0), (0, 1), (0, 0)))

def centred_conv3(x, w, b):
    return shift_prev(x) * w[0] + x * w[1] + shift_next(x) * w[2] + b

def swiglu(h, w1, w3, w2):
    return (jax.nn.silu(h @ w1) * (h @ w3)) @ w2

def neighbourhood_attention(q, k, v, kc, vc, rpb):
    B, L, H, Dh = q.shape
    rows = L // GRID_W
    kh = min(NA_MAX_ROWS, rows)
    qg = (q * (Dh ** -0.5)).reshape(B, rows, GRID_W, H, Dh)
    kg = k.reshape(B, rows, GRID_W, H, Dh)
    vg = v.reshape(B, rows, GRID_W, H, Dh)
    col = jnp.arange(GRID_W)
    col_start = jnp.clip(col - NA_COLS // 2, 0, GRID_W - NA_COLS)
    col_idx = col_start[:, None] + jnp.arange(NA_COLS)[None, :]
    col_rel = col_idx - col[:, None] + (NA_COLS - 1)

    def one_row(r):
        r0 = jnp.clip(r - kh // 2, 0, rows - kh)
        q_r = lax.dynamic_index_in_dim(qg, r, axis=1, keepdims=False)
        k_win = jnp.take(lax.dynamic_slice_in_dim(kg, r0, kh, axis=1), col_idx, axis=2)
        v_win = jnp.take(lax.dynamic_slice_in_dim(vg, r0, kh, axis=1), col_idx, axis=2)
        row_rel = r0 + jnp.arange(kh) - r + (NA_MAX_ROWS - 1)
        bias = rpb[:, row_rel[:, None, None], col_rel[None]].astype(jnp.float32)
        s_loc = jnp.einsum('bqhd,biqjhd->bhqij', q_r, k_win, preferred_element_type=jnp.float32)
        s_loc = s_loc + jnp.transpose(bias, (0, 2, 1, 3))[None]
        s_ctx = jnp.einsum('bqhd,bchd->bhqc', q_r, kc, preferred_element_type=jnp.float32)
        logits = jnp.concatenate([s_loc.reshape(B, H, GRID_W, kh * NA_COLS), s_ctx], axis=-1)
        p = jax.nn.softmax(logits, axis=-1).astype(v.dtype)
        p_loc = p[..., :kh * NA_COLS].reshape(B, H, GRID_W, kh, NA_COLS)
        out = jnp.einsum('bhqij,biqjhd->bqhd', p_loc, v_win) + jnp.einsum('bhqc,bchd->bqhd', p[..., kh * NA_COLS:], vc)
        return out.reshape(B, GRID_W, H * Dh)

    out = lax.map(one_row, jnp.arange(rows))
    return jnp.moveaxis(out, 0, 1).reshape(B, L, H * Dh)

def context_attention(qc, kc, vc):
    B, C, H, Dh = qc.shape
    s = jnp.einsum('bqhd,bkhd->bhqk', qc, kc, preferred_element_type=jnp.float32) * (Dh ** -0.5)
    p = jax.nn.softmax(s, axis=-1).astype(vc.dtype)
    return jnp.einsum('bhqk,bkhd->bqhd', p, vc).reshape(B, C, H * Dh)

def hyena_kernels_f(L, pw1, pb1, pw2, pb2, pw3, freq):
    f32 = jnp.float32
    pos = jnp.arange(L, dtype=f32)
    t = jnp.linspace(0.0, 1.0, L, dtype=f32)
    ang = (2.0 * math.pi / L) * pos[:, None] * jnp.linspace(1e-4, HY_BANDS - 1, HY_BANDS, dtype=f32)[None, :]
    z = jnp.concatenate([t[:, None], jnp.cos(ang), -jnp.sin(ang)], axis=-1)
    fr = freq.astype(f32)
    hid = jnp.sin(fr * (z @ pw1.astype(f32) + pb1.astype(f32)))
    hid = jnp.sin(fr * (hid @ pw2.astype(f32) + pb2.astype(f32)))
    h = (hid @ pw3.astype(f32)).reshape(L, 2, HY_ORDER, HY_WIDTH)
    deltas = jnp.abs(jnp.linspace(HY_MIN_DECAY, HY_MAX_DECAY, HY_WIDTH, dtype=f32))
    h = h * jnp.exp(-t[:, None] * deltas[None, :])[:, None, None, :]
    k_two = jnp.concatenate([h[:, 0], jnp.zeros((1, HY_ORDER, HY_WIDTH), f32), h[:0:-1, 1]], axis=0)
    k_two = k_two / jnp.sum(jnp.abs(k_two), axis=0, keepdims=True)
    return jnp.fft.rfft(k_two, axis=0)

def hyena(u, sw, sb, pw1, pb1, pw2, pb2, pw3, freq, skip):
    B, L, _ = u.shape
    u = centred_conv3(u, sw, sb)
    v, x1, x2 = jnp.split(u, 3, axis=-1)
    kf = hyena_kernels_f(L, pw1, pb1, pw2, pb2, pw3, freq)
    z = v
    for o, gate in enumerate((x1, x2)):
        zf = jnp.fft.rfft(z.astype(jnp.float32), n=2 * L, axis=1)
        conv = jnp.fft.irfft(zf * kf[None, :, o], n=2 * L, axis=1)[:, :L]
        z = gate * (conv.astype(z.dtype) + skip[o] * z)
    return z

def na_hyena_mixer(h, hc, w_in, w_out, rpb, sw, sb, pw1, pb1, pw2, pb2, pw3, freq, skip, ctx_out):
    B, L, _ = h.shape
    C = hc.shape[1]
    A = NA_WIDTH
    heads = lambda t, n: t.reshape(B, n, NA_HEADS, NA_HEAD_DIM)
    p = h @ w_in
    q, k, v = heads(p[..., :A], L), heads(p[..., A:2 * A], L), heads(p[..., 2 * A:3 * A], L)
    kvc = hc @ w_in[:, A:3 * A]
    kc, vc = heads(kvc[..., :A], C), heads(kvc[..., A:], C)
    hy_args = (sw, sb, pw1, pb1, pw2, pb2, pw3, freq, skip)
    y = jnp.concatenate([neighbourhood_attention(q, k, v, kc, vc, rpb), hyena(p[..., 3 * A:], *hy_args)], axis=-1) @ w_out
    if not ctx_out:
        return y, None
    qc = heads(hc @ w_in[:, :A], C)
    yc = jnp.concatenate([context_attention(qc, kc, vc), hyena(hc @ w_in[:, 3 * A:], *hy_args)], axis=-1) @ w_out
    return y, yc

def rw_heads(t):
    return t.reshape(t.shape[:-1] + (RW_HEADS, RW_HEAD))

def rwkv_features(h, mu, w_rkv, w0, w1, w2, a0, a1, a2, g1, g2, k_k, k_a, readout):
    xx = 0.5 * (shift_prev(h) + shift_next(h)) - h
    mix = lambda i: h + xx * mu[i]
    xw, xa = mix(1), mix(4)
    k = mix(2) @ w_rkv[1]
    v = mix(3) @ w_rkv[2]
    lw = jnp.einsum('eblr,erd->ebld', jnp.tanh(jnp.einsum('bld,edr->eblr', xw, w1)), w2) + w0[:, None, None, :]
    decay = jnp.exp(-jnp.exp(-jax.nn.softplus(-lw.astype(jnp.float32)) - 0.5))
    a = jax.nn.sigmoid(jnp.einsum('eblr,erd->ebld', jnp.einsum('bld,edr->eblr', xa, a1), a2) + a0[:, None, None, :])
    kk = rw_heads(k * k_k).astype(jnp.float32)
    kk = kk / jnp.maximum(jnp.sqrt(jnp.sum(jnp.square(kk), axis=-1, keepdims=True)), 1e-12)
    k_dir = k[None] * (1.0 + (a - 1.0) * k_a)
    if readout:
        r = mix(0) @ w_rkv[0]
        g = jax.nn.sigmoid(mix(5) @ g1) @ g2
    else:
        r = None
        g = None
    return r, decay, k_dir, v, kk, a, g

def wkv_scan(s0, decay, k, v, kk, a, r):
    tm = lambda t: jnp.moveaxis(t, 2, 0)

    def update(s, w_t, k_t, v_t, kk_t, a_t):
        sa = jnp.einsum('ebhvk,ebhk->ebhv', s, kk_t)
        return s * w_t[..., None, :] - sa[..., :, None] * (kk_t * a_t)[..., None, :] + v_t[..., :, None] * k_t[..., None, :]

    xs = tuple(tm(t) for t in (decay, k, v, kk, a))
    if r is None:
        s, _ = lax.scan(lambda s, inp: (update(s, *inp), None), s0, xs)
        return s, None

    def step(s, inp):
        s = update(s, *inp[:5])
        return s, jnp.einsum('ebhvk,ebhk->ebhv', s, inp[5])

    s, ys = lax.scan(step, s0, xs + (tm(r),))
    return s, jnp.moveaxis(ys, 0, 2)

def rwkv_run_scan(s0, r, decay, k_dir, v, kk, a):
    f32 = jnp.float32
    per_dir = lambda t: jnp.stack([t[0], jnp.flip(t[1], axis=1)]).astype(f32)
    shared = lambda t: jnp.stack([t, jnp.flip(t, axis=1)]).astype(f32)
    rr = None if r is None else shared(rw_heads(r))
    s, y = wkv_scan(s0, per_dir(rw_heads(decay)), per_dir(rw_heads(k_dir)), shared(rw_heads(v)), shared(kk), per_dir(rw_heads(a)), rr)
    if y is not None:
        y = y[0] + jnp.flip(y[1], axis=1)
    return s, y

def rwkv_output(y, r, k_dir, v, g, r_k, ln_w, ln_b, w_o):
    B, L, H, N = y.shape
    f32 = jnp.float32
    mean = jnp.mean(y, axis=-1, keepdims=True)
    var = jnp.mean(jnp.square(y - mean), axis=-1, keepdims=True)
    yn = ((y - mean) * lax.rsqrt(var + RW_GN_EPS)).reshape(B, L, H * N) * ln_w.astype(f32) + ln_b.astype(f32)
    coef = jnp.sum(rw_heads(r).astype(f32)[None] * rw_heads(k_dir).astype(f32) * r_k[:, None, None].astype(f32), axis=(0, -1))[..., None]
    bonus = (coef * rw_heads(v).astype(f32)).reshape(B, L, H * N)
    return ((yn + bonus).astype(v.dtype) * g) @ w_o

def rwkv_mixer(h, hc, mu, w_rkv, w_o, w0, w1, w2, a0, a1, a2, g1, g2, k_k, k_a, r_k, ln_w, ln_b, ctx_out):
    B = h.shape[0]
    fa = (mu, w_rkv, w0, w1, w2, a0, a1, a2, g1, g2, k_k, k_a)
    rc, dc, kc, vc, kkc, ac, gc = rwkv_features(hc, *fa, readout=ctx_out)
    r, d, kd, v, kk, a, g = rwkv_features(h, *fa, readout=True)
    s0 = jnp.zeros((2, B, RW_HEADS, RW_HEAD, RW_HEAD), jnp.float32)
    s_ctx, y_ctx = rwkv_run_scan(s0, rc, dc, kc, vc, kkc, ac)
    _, y_lat = rwkv_run_scan(s_ctx, r, d, kd, v, kk, a)
    out = rwkv_output(y_lat, r, kd, v, g, r_k, ln_w, ln_b, w_o)
    out_c = rwkv_output(y_ctx, rc, kc, vc, gc, r_k, ln_w, ln_b, w_o) if ctx_out else None
    return out, out_c

def setup_inputs(seed: int = 0) -> dict:
    key = jax.random.key(seed)
    ks = iter(jax.random.split(key, 48))
    nrm = lambda shape, s: jax.random.normal(next(ks), shape, jnp.float32) * s
    D, F, NE, NO = D_MODEL, FFN_HIDDEN, N_EVEN, N_ODD
    return {
        'x': nrm((BATCH, SEQ, D), 1.0),
        'c': nrm((BATCH, D), 1.0),
        'ctx': nrm((BATCH, CTX_LEN, D), 1.0),
        'c_ctx': nrm((D,), 1.0),
        'mod_w': nrm((DEPTH, D, 6 * D), 0.5 * D ** -0.5),
        'mod_b': nrm((DEPTH, 6 * D), 0.02),
        'norm_g': 1.0 + nrm((DEPTH, 4, D), 0.05),
        'ffn_w1': nrm((DEPTH, D, F), D ** -0.5),
        'ffn_w3': nrm((DEPTH, D, F), D ** -0.5),
        'ffn_w2': nrm((DEPTH, F, D), F ** -0.5),
        'mix_w_in': nrm((NE, D, EVEN_IN), D ** -0.5),
        'mix_w_out': nrm((NE, NA_WIDTH + HY_WIDTH, D), (NA_WIDTH + HY_WIDTH) ** -0.5),
        'na_rpb': nrm((NE, NA_HEADS, 2 * NA_MAX_ROWS - 1, 2 * NA_COLS - 1), 0.1),
        'hy_short_w': nrm((NE, HY_SHORT, 3 * HY_WIDTH), HY_SHORT ** -0.5),
        'hy_short_b': nrm((NE, 3 * HY_WIDTH), 0.02),
        'hy_pos_w1': nrm((NE, HY_EMB, HY_FFN), HY_EMB ** -0.5),
        'hy_pos_b1': nrm((NE, HY_FFN), 0.1),
        'hy_pos_w2': nrm((NE, HY_FFN, HY_FFN), HY_FFN ** -0.5),
        'hy_pos_b2': nrm((NE, HY_FFN), 0.1),
        'hy_pos_w3': nrm((NE, HY_FFN, 2 * HY_ORDER * HY_WIDTH), HY_FFN ** -0.5),
        'hy_sin_freq': 1.0 + nrm((NE, HY_FFN), 0.05),
        'hy_skip': nrm((NE, HY_ORDER, HY_WIDTH), 1.0),
        'rw_mu': jax.random.uniform(next(ks), (NO, 6, D), jnp.float32),
        'rw_w_rkv': nrm((NO, 3, D, D), D ** -0.5),
        'rw_w_o': nrm((NO, D, D), D ** -0.5),
        'rw_w0': jax.random.uniform(next(ks), (NO, 2, D), jnp.float32, -6.0, -1.0),
        'rw_w1': nrm((NO, 2, D, RW_DECAY_LORA), D ** -0.5),
        'rw_w2': nrm((NO, 2, RW_DECAY_LORA, D), 0.5 * RW_DECAY_LORA ** -0.5),
        'rw_a0': nrm((NO, 2, D), 0.5),
        'rw_a1': nrm((NO, 2, D, RW_AAA_LORA), D ** -0.5),
        'rw_a2': nrm((NO, 2, RW_AAA_LORA, D), 0.5 * RW_AAA_LORA ** -0.5),
        'rw_g1': nrm((NO, D, RW_GATE_LORA), D ** -0.5),
        'rw_g2': nrm((NO, RW_GATE_LORA, D), RW_GATE_LORA ** -0.5),
        'rw_k_k': 0.85 + nrm((NO, D), 0.05),
        'rw_k_a': 1.0 + nrm((NO, D), 0.05),
        'rw_r_k': nrm((NO, 2, RW_HEADS, RW_HEAD), 0.1),
        'rw_ln_w': 1.0 + nrm((NO, D), 0.05),
        'rw_ln_b': nrm((NO, D), 0.02),
    }

def reference(x, c, ctx, c_ctx, mod_w, mod_b, norm_g, ffn_w1, ffn_w3, ffn_w2, mix_w_in, mix_w_out, na_rpb, hy_short_w, hy_short_b, hy_pos_w1, hy_pos_b1, hy_pos_w2, hy_pos_b2, hy_pos_w3, hy_sin_freq, hy_skip, rw_mu, rw_w_rkv, rw_w_o, rw_w0, rw_w1, rw_w2, rw_a0, rw_a1, rw_a2, rw_g1, rw_g2, rw_k_k, rw_k_a, rw_r_k, rw_ln_w, rw_ln_b):
    xc = ctx
    for layer in range(DEPTH):
        last = layer == DEPTH - 1
        g = norm_g[layer]
        m = (jax.nn.silu(c) @ mod_w[layer] + mod_b[layer])[:, None, :]
        sh_a, sc_a, ga, sh_f, sc_f, gf = jnp.split(m, 6, axis=-1)
        mc = jax.nn.silu(c_ctx) @ mod_w[layer] + mod_b[layer]
        csh_a, csc_a, cga, csh_f, csc_f, cgf = jnp.split(mc, 6, axis=-1)
        h = rms_norm(x, g[0]) * (1.0 + sc_a) + sh_a
        hc = rms_norm(xc, g[0]) * (1.0 + csc_a) + csh_a
        j = layer // 2
        if layer % 2 == 0:
            y, yc = na_hyena_mixer(h, hc, mix_w_in[j], mix_w_out[j], na_rpb[j], hy_short_w[j], hy_short_b[j], hy_pos_w1[j], hy_pos_b1[j], hy_pos_w2[j], hy_pos_b2[j], hy_pos_w3[j], hy_sin_freq[j], hy_skip[j], not last)
        else:
            y, yc = rwkv_mixer(h, hc, rw_mu[j], rw_w_rkv[j], rw_w_o[j], rw_w0[j], rw_w1[j], rw_w2[j], rw_a0[j], rw_a1[j], rw_a2[j], rw_g1[j], rw_g2[j], rw_k_k[j], rw_k_a[j], rw_r_k[j], rw_ln_w[j], rw_ln_b[j], not last)
        x = x + ga * rms_norm(y, g[1])
        f = rms_norm(x, g[2]) * (1.0 + sc_f) + sh_f
        x = x + gf * rms_norm(swiglu(f, ffn_w1[layer], ffn_w3[layer], ffn_w2[layer]), g[3])
        if not last:
            xc = xc + cga * rms_norm(yc, g[1])
            fc = rms_norm(xc, g[2]) * (1.0 + csc_f) + csh_f
            xc = xc + cgf * rms_norm(swiglu(fc, ffn_w1[layer], ffn_w3[layer], ffn_w2[layer]), g[3])
    return x


_drawn_inputs = setup_inputs


def setup_inputs(seed=0):
    import zlib

    import numpy as np

    out = dict(_drawn_inputs(seed))
    spreads = {}
    factors = {'na_rpb': 23.196,
     'hy_short_b': 5.093,
     'hy_pos_b1': 3.704,
     'hy_pos_b2': 3.731,
     'hy_sin_freq': 8.0,
     'rw_w1': 4.368,
     'rw_w2': 4.551,
     'rw_ln_w': 14.913,
     'rw_ln_b': 39.598,
     'rw_r_k': 2.813}
    for name, (base, spread) in spreads.items():
        noise = np.random.default_rng([zlib.crc32(name.encode()), seed]).standard_normal(out[name].shape)
        drawn = base * np.exp(spread * noise) if base else spread * noise
        out[name] = __import__('jax').numpy.asarray(drawn.astype(out[name].dtype))
    for name, factor in factors.items():
        out[name] = (out[name] * factor).astype(out[name].dtype)
    return out
```

```python
import concourse.bass as bass
from concourse import mybir
from contextlib import ExitStack
import numpy as np
import math

F32 = mybir.dt.float32
ALU = mybir.AluOpType
ACT = mybir.ActivationFunctionType
AX_X = mybir.AxisListType.X

D = 1024
L = 512
C = 256
T = L + C
CT = D // 128
F = 2816
FT = F // 128
HALF = T // 2
GRID = 64
ROWS = L // GRID
WIN = 16
NH = 8
HW = 512
ORD = 2
EMB = 33
HID = 64
RH = 16
CH = 64
DLORA = 64
GLORA = 160
EPS = 1e-6
GN_EPS = 64e-5
PI = math.pi
SLOTS = 4
SLOT_K = 11
HP = T + 3


def shape_constants():
    f4 = np.float32
    t = {}
    i = np.arange(128)
    t["ident"] = np.eye(128, dtype=f4)
    t["ones"] = np.full((128, 128), 1.0 / D, f4)
    t["headones"] = (i[:, None] // 64 == i[None, :] // 64).astype(f4)
    u = np.zeros((64, 3 * GRID - 1), f4)
    for m in range(2 * WIN - 1):
        for r in range(2):
            u[32 * r + m, GRID * (r + 1) + WIN - 2 - m] = 1.0
    t["pick"] = u
    col = np.arange(GRID)
    start = np.clip(col - WIN // 2, 0, GRID - WIN)
    inside = (col[None, :] >= start[:, None]) & (col[None, :] < start[:, None] + WIN)
    t["window"] = np.tile(np.where(inside, 0.0, -1e30), (2, 1)).astype(f4)
    for n in (L, C):
        th = np.pi * np.outer(np.arange(n), 2 * np.arange(n) + 1) / (2 * n)
        m = np.stack([np.cos(th), np.sin(th), np.cos(th).T / n, np.sin(th).T / n])
        t[f"dft{n}"] = np.ascontiguousarray(
            m.reshape(4, n // 128, 128, n).transpose(2, 0, 1, 3)).astype(f4)
    bands = (EMB - 1) // 2
    feats, cols = [], []
    for n in (L, C):
        pos = np.arange(n, dtype=f4)
        tt = np.linspace(0.0, 1.0, n, dtype=f4)
        ang = f4(2.0 * math.pi / n) * pos[:, None] * np.linspace(1e-4, bands - 1, bands, dtype=f4)[None, :]
        feats.append(np.concatenate([tt[:, None], np.cos(ang), -np.sin(ang)], -1).T)
        c = -tt.reshape(n // 128, 128).T
        back = c.copy()
        back[0, 0] = -1e4
        cols += [c, back]
    t["feats"] = np.concatenate(feats, 1).astype(f4)
    t["times"] = np.concatenate(cols, 1).astype(f4)
    lo, hi = math.log(1e-2) / 1.5, math.log(1e-2) / 0.3
    t["deltas"] = np.tile(np.abs(np.linspace(lo, hi, HW, dtype=f4))[None], (128, 1))
    s, q = np.arange(64)[:, None], np.arange(64)[None, :]
    gram = []
    for strict, incl in (((s < q), (s <= q)), ((s > q), (s >= q))):
        one = np.concatenate([strict, incl, strict, incl], 1)
        gram.append(np.concatenate([one, one], 1))
    t["grammask"] = np.tile(np.stack(gram, 1), (2, 1, 1)).astype(f4)
    lev = []
    for m in (1, 2, 4, 8, 16, 32):
        same = (s // (2 * m)) == (q // (2 * m))
        later = same & (s % (2 * m) >= m) & (q % (2 * m) < m)
        lev.append([later, later.T])
    lev = np.array(lev).astype(f4)
    t["levelmask"] = np.ascontiguousarray(np.tile(lev.transpose(2, 0, 1, 3), (2, 1, 1, 1)))
    t["eye2"] = np.tile(np.eye(64, dtype=f4), (2, 1))
    run = np.ones((128, T), f4)
    run[:, ::64] = 0.0
    t["run"] = run
    return t


def hybrid_dit_kernel(nc, a, out):
    ctx = ExitStack()
    with ctx:
        def sb(name, shape, dt=F32):
            return ctx.enter_context(nc.sbuf_tensor(name, shape, dt))

        def sem(name):
            return ctx.enter_context(nc.semaphore(name))

        PS = ctx.enter_context(nc.psum_tensor("PS", [128, 8, 512], F32))

        NROWS = (80, 96, 104, 80)
        PBASE = (0, 80, 176, 280)

        X = sb("X", [128, CT, T])
        Hraw = sb("Hraw", [128, CT * HP])
        H = Hraw[:, 0:CT * T].rearrange("p (c t) -> p c t", c=CT)
        Hpad = Hraw[:, :].rearrange("p (c t) -> p c t", c=CT)
        Y = sb("Y", [128, CT, T])
        Yf = Y[:, :, :].rearrange("p c t -> p (c t)")
        P = sb("P", [128, 24, T])
        Pf = P[:, :, :].rearrange("p c t -> p (c t)")
        WR = sb("WR", [128, SLOTS, SLOT_K, 128])
        WRf = WR[:, :, :, :].rearrange("p s k m -> p (s k m)")
        TMPN = 9624
        TMP = sb("TMP", [128, TMPN])
        ident = sb("ident", [128, 128])
        ones = sb("ones", [128, 128])
        PC = sb("PC", [128, sum(NROWS)])
        modT = sb("modT", [128, 2, 48, 2])
        DER = sb("DER", [128, 2, 4, 2, 8])
        small = sb("small", [128, 64])

        def carve(base, sizes):
            views, at = [], 0
            for n in sizes:
                views.append(base[:, at:at + n])
                at += n
            assert at <= base.shape[1], (at, base.shape)
            return views

        def col(k):
            return PC[:, k:k + 1]

        G_COL = lambda l, k, t: 16 + (l * 4 + k) * 8 + t
        SW_COL, SB_COL, SKIP_COL, MU_COL = (PBASE[2] + x for x in (0, 36, 48, 56))
        W0_COL, A0_COL, KK_COL, KA_COL, RK_COL, LNW_COL, LNB_COL = (PBASE[3] + x for x in (0, 16, 32, 40, 48, 64, 72))

        def halves(bank, n=T):
            if n == T:
                return PS[:, bank:bank + 2, 0:HALF]
            return PS[:, bank, 0:n]

        def as_halves(ap, n=T):
            return ap.rearrange("p (h t) -> p h t", h=2) if n == T else ap

        def segs(n=T):
            return ((0, L, 0), (L, T, 1)) if n == T else ((0, L, 0),)

        consts_in = sem("consts_in")
        params_in = sem("params_in")
        x_in = sem("x_in")
        params_T = sem("params_T")
        params_ready = sem("params_ready")
        x_T = sem("x_T")
        x_evicted = sem("x_evicted")
        c_silu = sem("c_silu")
        mod_full = [sem(f"mod_full{s}") for s in range(3)]
        mod_mm = sem("mod_mm")
        mod_row = sem("mod_row")
        mod_cols = sem("mod_cols")
        mod_added = sem("mod_added")
        gains_ready = sem("gains_ready")
        w_full = [sem(f"w_full{s}") for s in range(SLOTS)]
        slots_used = sem("slots_used")
        sq_ready = sem("sq_ready")
        sq_used = sem("sq_used")
        root_ready = sem("root_ready")
        rstd_ready = sem("rstd_ready")
        scaled = sem("scaled")
        normed = sem("normed")
        x_updated = sem("x_updated")
        dve_step = sem("dve_step")
        act_step = sem("act_step")
        out_T = sem("out_T")
        out_sb = sem("out_sb")
        stored = sem("stored")

        SQ, ROOT, SCL, GATE, _ = carve(TMP, [2 * T, T, 2 * T, 2 * T, 0])
        SQ = SQ.rearrange("p (s t) -> p s t", s=2)
        SCL = SCL.rearrange("p (s t) -> p s t", s=2)
        GATE = GATE.rearrange("p (s t) -> p s t", s=2)

        class Dense:
            def __init__(self, name, kind, groups, base, w, rhs, dest, n=T):
                self.kind, self.groups, self.base, self.w, self.rhs, self.dest, self.n = \
                    kind, groups, base, w, rhs, dest, n
                self.units = 4 if kind == "plain" else 2
                self.unit_free = sem(name + "_banks_free")
                self.done = groups * self.units + self.units

        def tile_of_weights(w, m, k0, k1):
            v = w.rearrange("(k p) (m c) -> m p k c", p=128, c=128)
            return v[bass.ds(m, 1), :, k0:k1, :].rearrange("a p k c -> (a p) k c")

        def dense_load(sp, d, first=False):
            def group(i, wait):
                for s in range(SLOTS):
                    if wait:
                        sp.wait_ge(slots_used, 4 * (d.base - 1) + 4 * i + s + 1)
                    if d.kind == "plain":
                        sp.dma_start(WR[:, s, 0:CT, :], tile_of_weights(d.w, 4 * i + s, 0, CT))\
                          .then_inc(w_full[s], 16)
                    elif d.kind == "gate":
                        sp.dma_start(WR[:, s, 0:CT, :], tile_of_weights(d.w[s % 2], 2 * i + s // 2, 0, CT))\
                          .then_inc(w_full[s], 16)
                    else:
                        k0 = SLOT_K * (s % 2)
                        sp.dma_start(WR[:, s, :, :], tile_of_weights(d.w, 2 * i + s // 2, k0, k0 + SLOT_K))\
                          .then_inc(w_full[s], 16)
            if first:
                group(0, False)
            with sp.Fori(1 if first else 0, d.groups) as i:
                group(i, True)

        def dense_pe(pe, d):
            with pe.Fori(0, d.groups) as i:
                for s in range(SLOTS):
                    u = s if d.kind == "plain" else s // 2
                    bank = 2 * s if d.kind != "long" else 4 * u
                    begins = d.kind != "long" or s % 2 == 0
                    ends = d.kind != "long" or s % 2 == 1
                    if d.kind == "plain" or s % 2 == 0:
                        pe.wait_ge(d.unit_free, d.units * i + u + 1)
                    pe.wait_ge(w_full[s], 16 * (i + d.base + 1))
                    k0, kn = (SLOT_K * (s % 2), SLOT_K) if d.kind == "long" else (0, CT)
                    for k in range(kn):
                        for h0, h1, b in (((0, HALF, 0), (HALF, T, 1)) if d.n == T else ((0, L, 0),)):
                            last = nc.tensor.matmul(
                                PS[:, bank + b, 0:h1 - h0], WR[:, s, k, :], d.rhs(k0 + k)[:, h0:h1],
                                start=begins and k == 0, stop=ends and k == kn - 1)
                    last.then_inc(slots_used, 1)

        def dense_evict_act(act, d):
            if d.kind != "gate":
                act.sem_inc(d.unit_free, d.units)
            with act.Fori(0, d.groups) as i:
                for u in range(d.units):
                    last_slot = u if d.kind == "plain" else (2 * u if d.kind == "gate" else 2 * u + 1)
                    bank = 2 * u if d.kind == "plain" else 4 * u
                    act.wait_ge(slots_used, 4 * d.base + 4 * i + last_slot + 1)
                    if d.kind == "gate":
                        nc.scalar.activation(as_halves(GATE[:, u, 0:d.n], d.n), halves(bank, d.n), ACT.Silu)\
                          .then_inc(silu_ready, 1)
                    else:
                        act.wait_ge(consts_in, CONST_DMAS)
                        dst = d.dest[:, bass.ds(d.units * i + u, 1), 0:d.n].rearrange("p a t -> p (a t)")
                        nc.scalar.activation(as_halves(dst, d.n), halves(bank, d.n), ACT.Copy)\
                          .then_inc(d.unit_free, 1)

        def gate_evict_dve(v, d, silu_base):
            v.sem_inc(d.unit_free, d.units)
            with v.Fori(0, d.groups) as i:
                for u in range(2):
                    v.wait_ge(slots_used, 4 * d.base + 4 * i + 2 * u + 2)
                    v.wait_ge(silu_ready, silu_base + 2 * i + u + 1)
                    dst = d.dest[:, bass.ds(2 * i + u, 1), 0:d.n].rearrange("p a t -> p (a t)")
                    nc.vector.tensor_tensor(as_halves(dst, d.n), as_halves(GATE[:, u, 0:d.n], d.n),
                                            halves(4 * u + 2, d.n), ALU.mult).then_inc(d.unit_free, 1)

        silu_ready = sem("silu_ready")

        def norm_squares_act(act, q, src, n, ready):
            for t in range(CT):
                ready(act, t)
                if t >= 2 or q > 0:
                    act.wait_ge(sq_used, q * CT + t - 1)
                nc.scalar.activation(SQ[:, t % 2, 0:n], src(t), ACT.Square).then_inc(sq_ready, 1)
            act.wait_ge(sq_used, q * CT + CT)
            nc.scalar.activation(as_halves(ROOT[:, 0:n], n), halves(0, n), ACT.Sqrt, bias=small[:, 0:1])\
              .then_inc(root_ready, 1)

        def norm_pe(pe, q, n, before):
            before(pe)
            for t in range(CT):
                pe.wait_ge(sq_ready, q * CT + t + 1)
                for h0, h1, b in (((0, HALF, 0), (HALF, T, 1)) if n == T else ((0, L, 0),)):
                    last = nc.tensor.matmul(PS[:, b, 0:h1 - h0], ones[:, :], SQ[:, t % 2, h0:h1],
                                            start=t == 0, stop=t == CT - 1)
                last.then_inc(sq_used, 1)

        def norm_scale_dve(v, q, src, n, scaled_base=None, residual=None):
            v.wait_ge(root_ready, q + 1)
            nc.vector.reciprocal(halves(2, n), as_halves(ROOT[:, 0:n], n)).then_inc(rstd_ready, 1)
            v.wait_ge(rstd_ready, q + 1)
            for t in range(CT):
                if residual is None and t >= 2:
                    v.wait_ge(normed, NORMED_BASE[q] + t - 1)
                ins = nc.vector.tensor_tensor(as_halves(SCL[:, t % 2, 0:n], n), as_halves(src(t), n),
                                              halves(2, n), ALU.mult)
                ins.then_inc(scaled, 1)
                if residual is not None:
                    v.wait_ge(scaled, q * CT + t + 1)
                    l, k = residual
                    for s0, s1, w in segs(n):
                        last = nc.vector.scalar_tensor_tensor(
                            X[:, t, s0:s1], SCL[:, t % 2, s0:s1], DER[:, l, k, w, t:t + 1], X[:, t, s0:s1],
                            ALU.mult, ALU.add)
                    last.then_inc(x_updated, 1)

        def norm_shift_act(act, q, n, l, k, dest):
            for t in range(CT):
                act.wait_ge(scaled, q * CT + t + 1)
                for s0, s1, w in segs(n):
                    j = (0 if k == 0 else 24) + t
                    last = nc.scalar.activation(dest(t, s0, s1), SCL[:, t % 2, s0:s1], ACT.Identity,
                                                bias=modT[:, l, j, w:w + 1], scale=DER[:, l, k, w, t:t + 1])
                last.then_inc(normed, 1)

        NORMED_BASE = {0: 0, 2: 8, 4: 16, 6: 24}

        class Chain:
            def __init__(self, eng, s, per=0):
                self.eng, self.s, self.per, self.k, self.turn = eng, s, per, 0, 0

            def start(self, i):
                assert i is None or self.k in (0, self.per), (self.k, self.per)
                self.turn, self.k = i * self.per, 0

            def link(self, ins):
                self.k += 1
                ins.then_inc(self.s, 1)
                self.eng.wait_ge(self.s, self.turn + self.k)

            def end(self):
                assert self.k == self.per, (self.k, self.per)

        passed = sem("passed")

        QP, KP, VP, VT, SC, ST = carve(WRf, [T, T, T, T, 2 * T, 16])
        SC = SC.rearrange("p (s t) -> p s t", s=2)
        VT = VT.rearrange("p (k c) -> p k c", k=6)
        ND = 2 * ROWS - 1
        BIAS, BP = carve(TMP, [NH * ND * GRID, 2 * ND * GRID])
        BIAS = BIAS.rearrange("p (x j) -> p x j", j=GRID)
        PT, PTC, RPL, RP, PICK, WINDOW = carve(Yf, [6 * L, 2 * C, 2 * WIN - 1, NH * ND, 3 * GRID - 1, GRID])
        PT = PT.rearrange("p (k t) -> p k t", k=6)
        PTC = PTC.rearrange("p (k t) -> p k t", k=2)
        ITEMS = [(hh, t) for hh in range(2) for t in range(6)]

        bias_in = sem("bias_in")
        rpb_T = sem("rpb_T")
        rpb_ready = sem("rpb_ready")
        bias_mm = sem("bias_mm")
        bias_ready = sem("bias_ready")
        pair_in = sem("pair_in")
        scores_done = sem("scores_done")
        max_ready = sem("max_ready")
        exp_done = sem("exp_done")
        probs_ready = sem("probs_ready")
        tr_done = sem("tr_done")
        tr_evicted = sem("tr_evicted")
        pv_done = sem("pv_done")
        attn_out = sem("attn_out")
        attn_step = sem("attn_step")

        def bias_pe(pe):
            pe.wait_ge(bias_in, 48)
            pe.wait_ge(inproj.unit_free, inproj.done)
            nc.tensor.transpose(PS[0:2 * WIN - 1, 0, 0:NH * ND], RPL[0:NH * ND, :], ident[0:NH * ND, 0:NH * ND])\
              .then_inc(rpb_T, 1)
            pe.wait_ge(rpb_ready, 3)
            for g in range(GRID // 4):
                if g >= 4:
                    pe.wait_ge(bias_ready, g - 3)
                for q in range(4):
                    j = 4 * g + q
                    last = nc.tensor.matmul(PS[:, 4 + g % 4, 120 * q:120 * q + 120],
                                            PICK[0:64, GRID - 1 - j:3 * GRID - 1 - j], RP[0:64, :],
                                            start=True, stop=True)
                last.then_inc(bias_mm, 1)

        def bias_dve(v):
            v.wait_ge(x_T, 8)
            v.wait_ge(x_evicted, 8)
            nc.vector.memset(RP[0:64, :], 0.0).then_inc(rpb_ready, 1)
            v.wait_ge(rpb_ready, 1)
            v.wait_ge(rpb_T, 1)
            rp = RP.rearrange("p (h d) -> p h d", h=NH)
            src = PS[0:2 * WIN - 1, 0, 0:NH * ND].rearrange("p (h d) -> p h d", h=NH)
            nc.vector.tensor_copy(rp[0:2 * WIN - 1, :, :], src).then_inc(rpb_ready, 1)
            nc.vector.tensor_copy(rp[32:32 + 2 * WIN - 1, :, 1:ND], src[:, :, 0:ND - 1]).then_inc(rpb_ready, 1)
            for g in range(GRID // 4):
                v.wait_ge(bias_mm, g + 1)
                w = WINDOW[:, 4 * g:4 * g + 4].unsqueeze(1).broadcast_to([128, 120, 4])
                nc.vector.tensor_tensor(BIAS[:, :, 4 * g:4 * g + 4],
                                        PS[:, 4 + g % 4, 0:480].rearrange("p (q x) -> p x q", q=4), w, ALU.add)\
                  .then_inc(bias_ready, 1)

        def attn_pool(pool):
            pool.wait_ge(inproj.unit_free, inproj.done)
            pool.wait_ge(bias_ready, GRID // 4)
            with pool.Fori(0, NH // 2) as i:
                pool.wait_ge(attn_out, 2 * i + 2)
                for dst, at in ((QP, 0), (KP, 4), (VP, 8)):
                    nc.gpsimd.tensor_copy(dst, P[:, bass.ds(at + i, 1), :].rearrange("p a t -> p (a t)"))\
                      .then_inc(pair_in, 1)
                nc.gpsimd.tensor_copy(BP.rearrange("p (x j) -> p x j", j=GRID),
                                      BIAS[:, bass.ds(2 * ND * i, 2 * ND), :]).then_inc(pair_in, 1)
                pool.wait_ge(pair_in, 5 * i + 4)
                pool.sem_inc(passed, 1)
                nc.gpsimd.tensor_scalar(QP, QP, CH ** -0.5, None, ALU.mult).then_inc(pair_in, 1)

        def attn_pe(pe):
            pe.sem_inc(tr_done, 2)
            pe.sem_inc(pv_done, 4)

            def scores(i, n):
                hh, t = ITEMS[n]
                r = slice(64 * hh, 64 * hh + 64)
                pe.wait_ge(exp_done, 12 * i + n + 1)
                if t < 4:
                    nc.tensor.matmul(PS[:, n % 2, 0:L], QP[r, 128 * t:128 * t + 128], KP[r, 0:L],
                                     start=True, stop=True)
                nc.tensor.matmul(PS[:, 2 + n % 2, 0:C], QP[r, 128 * t:128 * t + 128], KP[r, L:T],
                                 start=True, stop=True).then_inc(scores_done, 1)

            def transposes(i, n):
                hh, t = ITEMS[n]
                pe.wait_ge(tr_evicted, 13 * i + n + 2)
                pe.wait_ge(probs_ready, 12 * i + n + 1)
                for k in range(6 if t < 4 else 2):
                    at = 128 * k if t < 4 else L + 128 * k
                    last = nc.tensor.transpose(PS[:, 4 + k // 3, 128 * (k % 3):128 * (k % 3) + 128],
                                               SC[:, n % 2, at:at + 128], ident[:, :])
                last.then_inc(tr_done, 1)

            def latent_out(i, hh):
                if hh == 0:
                    pe.wait_ge(attn_out, 2 * i + 2)
                pe.wait_ge(tr_evicted, 13 * i + 6 * hh + 4 + 2)
                for k in range(6):
                    last = nc.tensor.matmul(PS[64 * hh:64 * hh + 64, 6, 0:L], VT[:, k, 64 * hh:64 * hh + 64],
                                            PT[:, k, :], start=k == 0, stop=k == 5)
                last.then_inc(pv_done, 1)

            def context_out(i, hh):
                pe.wait_ge(tr_evicted, 13 * i + 6 * hh + 6 + 2)
                for k in range(2):
                    last = nc.tensor.matmul(PS[64 * hh:64 * hh + 64, 7, 0:C], VT[:, 4 + k, 64 * hh:64 * hh + 64],
                                            PTC[:, k, :], start=k == 0, stop=k == 1)
                last.then_inc(pv_done, 1)

            with pe.Fori(0, NH // 2) as i:
                pe.wait_ge(pair_in, 5 * i + 5)
                scores(i, 0)
                pe.wait_ge(tr_evicted, 13 * i + 1)
                for k in range(6):
                    last = nc.tensor.transpose(PS[:, 4 + k // 3, 128 * (k % 3):128 * (k % 3) + 128],
                                               VP[:, 128 * k:128 * k + 128], ident[:, :])
                last.then_inc(tr_done, 1)
                for n in range(12):
                    if n < 11:
                        scores(i, n + 1)
                    transposes(i, n)
                    if n % 6 == 4:
                        latent_out(i, n // 6)
                    if n == 6:
                        context_out(i, 0)
                context_out(i, 1)

        def attn_act(act):
            act.sem_inc(exp_done, 2)
            act.sem_inc(tr_evicted, 1)

            def evict(i, n):
                hh, t = ITEMS[n]
                if t in (0, 4):
                    act.wait_ge(pv_done, 4 * i + (3 if t == 0 else 4) + 2 * hh)
                act.wait_ge(tr_done, 13 * i + n + 4)
                if t < 4:
                    nc.scalar.activation(PT[:, :, 128 * t:128 * t + 128].rearrange("p (h k) c -> p h k c", h=2),
                                         halves(4).rearrange("p h (k c) -> p h k c", k=3), ACT.Copy)\
                      .then_inc(tr_evicted, 1)
                else:
                    nc.scalar.activation(PTC[:, :, 128 * (t - 4):128 * (t - 4) + 128],
                                         PS[:, 4, 0:256].rearrange("p (k c) -> p k c", k=2), ACT.Copy)\
                      .then_inc(tr_evicted, 1)

            with act.Fori(0, NH // 2) as i:
                for n, (hh, t) in enumerate(ITEMS):
                    st = ST[:, 8 * (n % 2):8 * (n % 2) + 8]
                    act.wait_ge(max_ready, 12 * i + n + 1)
                    if t < 4:
                        nc.scalar.activation(SC[:, n % 2, 0:L], SC[:, n % 2, 0:L], ACT.Exp, bias=st[:, 2:3],
                                             accum_out=st[:, 3:4])
                    nc.scalar.activation(SC[:, n % 2, L:T], PS[:, 2 + n % 2, 0:C], ACT.Exp, bias=st[:, 2:3],
                                         accum_out=st[:, 4:5]).then_inc(exp_done, 1)
                    if n == 0:
                        act.wait_ge(tr_done, 13 * i + 3)
                        act.wait_ge(pv_done, 4 * i + 4)
                        nc.scalar.activation(VT[:, :, :].rearrange("p (h k) c -> p h k c", h=2),
                                             halves(4).rearrange("p h (k c) -> p h k c", k=3), ACT.Copy)\
                          .then_inc(tr_evicted, 1)
                    else:
                        evict(i, n - 1)
                evict(i, 11)

        ATTN_LINKS = 8 * 4 + 4 * 3

        def attn_dve(v):
            v.sem_inc(attn_out, 2)
            chain = Chain(v, attn_step, ATTN_LINKS)

            def maximum(i, n):
                hh, t = ITEMS[n]
                st = ST[:, 8 * (n % 2):8 * (n % 2) + 8]
                v.wait_ge(scores_done, 12 * i + n + 1)
                v.wait_ge(tr_done, 13 * i + n + (2 if n >= 2 else 1))
                v.sem_inc(passed, 1)
                if t < 4:
                    bp = BP[:, (hh * ND + 7 - 2 * t) * GRID:(hh * ND + 15 - 2 * t) * GRID]
                    ins = nc.vector.tensor_tensor_reduce(
                        out=SC[:, n % 2, 0:L], in0=PS[:, n % 2, 0:L], in1=bp, scale=1.0, scalar=-3e38,
                        op0=ALU.add, op1=ALU.max, accum_out=st[:, 0:1])
                    chain.link(ins)
                    chain.link(nc.vector.reduce_max(st[:, 1:2], PS[:, 2 + n % 2, 0:C], AX_X))
                    nc.vector.scalar_tensor_tensor(st[:, 2:3], st[:, 0:1], st[:, 1:2], small[:, 1:2],
                                                   ALU.max, ALU.mult).then_inc(max_ready, 1)
                else:
                    chain.link(nc.vector.reduce_max(st[:, 1:2], PS[:, 2 + n % 2, 0:C], AX_X))
                    nc.vector.tensor_scalar(st[:, 2:3], st[:, 1:2], -1.0, None, ALU.mult).then_inc(max_ready, 1)

            def normalise(i, n):
                hh, t = ITEMS[n]
                st = ST[:, 8 * (n % 2):8 * (n % 2) + 8]
                v.wait_ge(exp_done, 12 * i + n + 3)
                if t < 4:
                    chain.link(nc.vector.tensor_tensor(st[:, 5:6], st[:, 3:4], st[:, 4:5], ALU.add))
                else:
                    chain.link(nc.vector.tensor_copy(st[:, 5:6], st[:, 4:5]))
                chain.link(nc.vector.reciprocal(st[:, 6:7], st[:, 5:6]))
                at = 0 if t < 4 else L
                nc.vector.tensor_scalar(SC[:, n % 2, at:T], SC[:, n % 2, at:T], st[:, 6:7], None, ALU.mult)\
                  .then_inc(probs_ready, 1)

            with v.Fori(0, NH // 2) as i:
                chain.start(i)
                v.wait_ge(pair_in, 5 * i + 5)
                maximum(i, 0)
                for n in range(12):
                    if n < 11:
                        maximum(i, n + 1)
                    normalise(i, n)
                v.wait_ge(pv_done, 4 * i + 8)
                for b, s0, s1 in ((6, 0, L), (7, L, T)):
                    nc.vector.tensor_scalar(H[:, bass.ds(i, 1), s0:s1].rearrange("p a t -> p (a t)"),
                                            PS[:, b, 0:s1 - s0], 1.0, None, ALU.mult).then_inc(attn_out, 1)
                chain.end()

        RUNS = [(L, 0, 0, 0), (L, 0, 1, 1), (C, L, 0, 2), (C, L, 1, 3)]
        CUM = [0, 4, 8, 10, 12]
        HYA = Pf[:, 12 * T:24 * T]
        HPM, ZT, T4, DEC = carve(HYA, [2 * 4 * HW, 4 * HW, 4 * HW, 2 * HW])
        HPM = HPM.rearrange("p (a k w) -> p a k w", a=2, k=4)
        YRI = HPM
        ZT = ZT.rearrange("p (k w) -> p k w", k=4)
        T4 = T4.rearrange("p (a w) -> p a w", a=4)
        DEC = DEC.rearrange("p (a w) -> p a w", a=2)
        DF, HIDT, DELTA, TIMES, PW1, PW2, PM, RN = carve(TMP, [8192, T, HW, 12, HID, HID, 4, 8])
        PW3, AB = carve(Yf, [4 * HW, 8 * HW])
        AB = AB.rearrange("p (a k w) -> p a k w", a=2, k=4)
        FEATS, ARG, KR = ZT[:, 0:2, :].rearrange("p k w -> p (k w)")[:, 0:T], \
            HPM[:, 0, 0:2, :].rearrange("p k w -> p (k w)")[:, 0:T], \
            HPM[:, 1, 0:2, :].rearrange("p k w -> p (k w)")[:, 0:T]
        HIDP = AB[:, 0, 0:2, :].rearrange("p k w -> p (k w)")[:, 0:T]

        def dft(n):
            return DF[:, 0:4 * (n // 128) * n].rearrange("p (a k f) -> p a k f", a=4, k=n // 128)

        hy_in = sem("hy_in")
        dft_in = sem("dft_in")
        feats_in = sem("feats_in")
        conv3_done = sem("conv3_done")
        conv3_step = sem("conv3_step")
        mlp_mm = sem("mlp_mm")
        mlp_arg = sem("mlp_arg")
        mlp_hid = sem("mlp_hid")
        filt_mm = sem("filt_mm")
        dec_ready = sem("dec_ready")
        hpm_ready = sem("hpm_ready")
        abs_ready = sem("abs_ready")
        sum_used = sem("sum_used")
        row_ready = sem("row_ready")
        rn_T = sem("rn_T")
        rn_ready = sem("rn_ready")
        ab_mm = sem("ab_mm")
        ab_ready = sem("ab_ready")
        zt_mm = sem("zt_mm")
        zt_ready = sem("zt_ready")
        z_mm = sem("z_mm")
        zmul_done = sem("zmul_done")
        y_ready = sem("y_ready")
        conv_mm = sem("conv_mm")
        z_done = sem("z_done")

        def hyena_sp(sp):
            sp.wait_ge(attn_out, 2 + NH)
            for dst, src in ((HIDT_IN[0], a["deltas"]), (TIMES, a["times"]), (PW1[0:EMB, :], a["hy_pos_w1"][0]),
                             (PW2[0:HID, :], a["hy_pos_w2"][0]), (PW3[0:HID, :], a["hy_pos_w3"][0]),
                             (PM[0:HID, 0:1], a["hy_pos_b1"].rearrange("a n -> n a")),
                             (PM[0:HID, 1:2], a["hy_pos_b2"].rearrange("a n -> n a")),
                             (PM[0:HID, 2:3], a["hy_sin_freq"].rearrange("a n -> n a"))):
                sp.dma_start(dst, src).then_inc(hy_in, 16)
            sp.dma_start(dft(L), a["dft512"]).then_inc(dft_in, 16)
            sp.wait_ge(conv3_done, 12)
            sp.dma_start(FEATS[0:EMB, :], a["feats"]).then_inc(feats_in, 16)
            sp.wait_ge(conv_mm, 8)
            sp.dma_start(dft(C), a["dft256"]).then_inc(dft_in, 16)

        HIDT_IN = [DELTA]

        def conv3_dve(v):
            chain = Chain(v, conv3_step, 2)
            v.wait_ge(params_ready, 4)
            with v.Fori(0, 12) as i:
                chain.start(i)
                src = P[:, bass.ds(12 + i, 1), :].rearrange("p a t -> p (a t)")
                dst = P[:, bass.ds(i, 1), :].rearrange("p a t -> p (a t)")

                def w(tap):
                    return PC[:, bass.ds(SW_COL + 12 * tap + i, 1)]
                chain.link(nc.vector.tensor_scalar(dst, src, w(1), PC[:, bass.ds(SB_COL + i, 1)], ALU.mult, ALU.add))
                for s0, s1, _ in segs():
                    ins = nc.vector.scalar_tensor_tensor(dst[:, s0 + 1:s1], src[:, s0:s1 - 1], w(0),
                                                         dst[:, s0 + 1:s1], ALU.mult, ALU.add)
                chain.link(ins)
                for s0, s1, _ in segs():
                    ins = nc.vector.scalar_tensor_tensor(dst[:, s0:s1 - 1], src[:, s0 + 1:s1], w(2),
                                                         dst[:, s0:s1 - 1], ALU.mult, ALU.add)
                ins.then_inc(conv3_done, 1)
                chain.end()

        def mlp_pe(pe):
            for k, (w, x) in enumerate(((PW1[0:EMB, :], FEATS[0:EMB, :]), (PW2[0:HID, :], HIDP[0:HID, :]))):
                pe.wait_ge(hy_in, 16 * 8)
                pe.wait_ge(feats_in, 16)
                if k:
                    pe.wait_ge(mlp_hid, 1)
                for h in range(2):
                    last = nc.tensor.matmul(PS[0:HID, h, 0:HALF], w, x[:, HALF * h:HALF * h + HALF],
                                            start=True, stop=True)
                last.then_inc(mlp_mm, 1)

        def mlp_dve(v, chain):
            for k in range(2):
                v.wait_ge(mlp_mm, k + 1)
                h = slice(0, HID)
                chain.link(nc.vector.tensor_scalar(as_halves(ARG[h, :]), PS[h, 0:2, 0:HALF], PM[h, k:k + 1],
                                                   PM[h, 2:3], ALU.add, ALU.mult))
                magic = 12582912.0
                chain.link(nc.vector.tensor_scalar(KR[h, :], ARG[h, :], 1.0 / (2 * PI), magic, ALU.mult, ALU.add))
                chain.link(nc.vector.tensor_scalar(KR[h, :], KR[h, :], magic, None, ALU.subtract))
                for c in (6.28125, 1.93500518798828125e-3, 3.0199159819e-7):
                    chain.link(nc.vector.scalar_tensor_tensor(ARG[h, :], KR[h, :], -c, ARG[h, :],
                                                              ALU.mult, ALU.add))
                nc.vector.tensor_scalar(ARG[h, :], ARG[h, :], 3.1415925, -3.1415925, ALU.min, ALU.max)\
                  .then_inc(mlp_arg, 1)

        def mlp_act(act):
            for k, dst in enumerate((HIDP, HIDT)):
                act.wait_ge(mlp_arg, k + 1)
                nc.scalar.activation(dst[0:HID, :], ARG[0:HID, :], ACT.Sin).then_inc(mlp_hid, 1)

        def hyena_pe(pe):
            for n, first, o, r in RUNS:
                nt, cum = n // 128, CUM[r]
                m = dft(n)
                pe.wait_ge(mlp_hid, 2)
                for k in range(nt):
                    if r:
                        pe.wait_ge(z_done, 4 * r)
                    if k >= 2:
                        pe.wait_ge(hpm_ready, cum + k - 1)
                    for d in range(2):
                        last = nc.tensor.matmul(
                            PS[:, 2 * (k % 2) + d, 0:HW], HIDT[0:HID, first + 128 * k:first + 128 * k + 128],
                            PW3[0:HID, (2 * d + o) * HW:(2 * d + o + 1) * HW], start=True, stop=True)
                    last.then_inc(filt_mm, 1)
                for k in range(nt):
                    pe.wait_ge(abs_ready, cum + k + 1)
                    for d in range(2):
                        last = nc.tensor.matmul(PS[0:1, 4, 0:HW], ones[:, 0:1], T4[:, 2 * (k % 2) + d, :],
                                                start=k + d == 0, stop=k == nt - 1 and d == 1)
                    last.then_inc(sum_used, 1)
                pe.wait_ge(dft_in, 16 if n == L else 32)
                pe.wait_ge(hpm_ready, cum + nt)
                for f in range(nt):
                    if f >= 2:
                        pe.wait_ge(ab_ready, cum + f - 1)
                    for p in range(2):
                        for k in range(nt):
                            last = nc.tensor.matmul(PS[:, 2 * (f % 2) + p, 0:HW], m[:, p, k, 128 * f:128 * f + 128],
                                                    HPM[:, p, k, :], start=k == 0, stop=k == nt - 1)
                    last.then_inc(ab_mm, 1)
                pe.wait_ge(row_ready, r + 1)
                for c in range(4):
                    last = nc.tensor.transpose(PS[:, 5, c:c + 1], DEC[0:1, 0, 128 * c:128 * c + 128], ident[0:1, 0:1])
                last.then_inc(rn_T, 1)
                for k in range(nt):
                    if k >= 2:
                        pe.wait_ge(zt_ready, cum + k - 1)
                    for c in range(4):
                        last = nc.tensor.transpose(PS[:, 6 + k % 2, 128 * c:128 * c + 128],
                                                   P[:, c, first + 128 * k:first + 128 * k + 128], ident[:, :])
                    last.then_inc(zt_mm, 1)
                pe.wait_ge(ab_ready, cum + nt)
                pe.wait_ge(zt_ready, cum + nt)
                for f in range(nt):
                    if f >= 2:
                        pe.wait_ge(zmul_done, cum + f - 1)
                    for p in range(2):
                        for k in range(nt):
                            last = nc.tensor.matmul(PS[:, 2 * (f % 2) + p, 0:HW], m[:, p, k, 128 * f:128 * f + 128],
                                                    ZT[:, k, :], start=k == 0, stop=k == nt - 1)
                    last.then_inc(z_mm, 1)
                pe.wait_ge(rn_ready, r + 1)
                pe.wait_ge(y_ready, cum + nt)
                for c in range(4):
                    for p in range(2):
                        for f in range(nt):
                            last = nc.tensor.matmul(PS[:, 4 + c, 0:n], YRI[:, p, f, 128 * c:128 * c + 128],
                                                    m[:, 2 + p, f, :], start=p + f == 0,
                                                    stop=p == 1 and f == nt - 1)
                    last.then_inc(conv_mm, 1)

        def hyena_act(act):
            act.wait_ge(hy_in, 16 * 8)
            for n, first, o, r in RUNS:
                nt, cum = n // 128, CUM[r]
                tcol = 0 if n == L else 8

                def decays(k):
                    if cum + k:
                        act.wait_ge(hpm_ready, cum + k)
                    if r and k == 0:
                        act.wait_ge(rn_T, r)
                    for d in range(2):
                        last = nc.scalar.activation(DEC[:, d, :], DELTA, ACT.Exp,
                                                    scale=TIMES[:, tcol + nt * d + k:tcol + nt * d + k + 1])
                    last.then_inc(dec_ready, 1)

                for k in range(nt):
                    decays(k)
                    act.wait_ge(hpm_ready, cum + k + 1)
                    for d in range(2):
                        x = T4[:, 2 * (k % 2) + d, :]
                        last = nc.scalar.activation(x, x, ACT.Abs)
                    last.then_inc(abs_ready, 1)
                for f in range(nt):
                    act.wait_ge(ab_mm, cum + f + 1)
                    nc.scalar.activation(AB[:, :, f, :], PS[:, 2 * (f % 2):2 * (f % 2) + 2, 0:HW], ACT.Copy)\
                      .then_inc(ab_ready, 1)
                for k in range(nt):
                    act.wait_ge(zt_mm, cum + k + 1)
                    nc.scalar.activation(ZT[:, k, :], PS[:, 6 + k % 2, 0:HW], ACT.Copy).then_inc(zt_ready, 1)

        def hyena_dve(v, chain):
            for n, first, o, r in RUNS:
                nt, cum = n // 128, CUM[r]
                for k in range(nt):
                    v.wait_ge(filt_mm, cum + k + 1)
                    v.wait_ge(dec_ready, cum + k + 1)
                    if k >= 2:
                        v.wait_ge(sum_used, cum + k - 1)
                    b = 2 * (k % 2)
                    chain.link(nc.vector.tensor_tensor(T4[:, b:b + 2, :], DEC[:, :, :], PS[:, b:b + 2, 0:HW], ALU.mult))
                    nc.vector.tensor_tensor(HPM[:, 0, k, :], T4[:, b, :], T4[:, b + 1, :], ALU.add)
                    nc.vector.tensor_tensor(HPM[:, 1, k, :], T4[:, b, :], T4[:, b + 1, :], ALU.subtract)\
                      .then_inc(hpm_ready, 1)
                v.wait_ge(sum_used, cum + nt)
                nc.vector.tensor_copy(DEC[0:1, 0, :], PS[0:1, 4, 0:HW]).then_inc(row_ready, 1)
                v.wait_ge(rn_T, r + 1)
                chain.link(nc.vector.reciprocal(RN[:, 4:8], PS[:, 5, 0:4]))
                nc.vector.tensor_scalar(RN[:, 0:4], RN[:, 4:8], 1.0 / D, None, ALU.mult).then_inc(rn_ready, 1)
                v.wait_ge(rn_ready, r + 1)
                v.wait_ge(ab_ready, cum + nt)
                for f in range(nt):
                    v.wait_ge(z_mm, cum + f + 1)
                    b = 2 * (f % 2)
                    if f:
                        v.wait_ge(y_ready, cum + f)
                    nc.vector.tensor_tensor(T4[:, 0:2, :], AB[:, :, f, :], PS[:, b:b + 2, 0:HW], ALU.mult)
                    for p in range(2):
                        ins = nc.vector.tensor_tensor(T4[:, 2 + p, :], AB[:, 1 - p, f, :], PS[:, b + p, 0:HW], ALU.mult)
                    ins.then_inc(zmul_done, 1)
                    v.wait_ge(zmul_done, cum + f + 1)
                    nc.vector.tensor_tensor(YRI[:, 0, f, :], T4[:, 0, :], T4[:, 1, :], ALU.subtract)
                    nc.vector.tensor_tensor(YRI[:, 1, f, :], T4[:, 2, :], T4[:, 3, :], ALU.add).then_inc(y_ready, 1)
                for c in range(4):
                    v.wait_ge(conv_mm, 4 * r + c + 1)
                    tmp = ZT[:, c, 0:n]
                    z = P[:, c, first:first + n]
                    gate = P[:, 4 + 4 * o + c, first:first + n]
                    chain.link(nc.vector.tensor_scalar(tmp, PS[:, 4 + c, 0:n], RN[:, c:c + 1], None, ALU.mult))
                    chain.link(nc.vector.scalar_tensor_tensor(tmp, z, col(SKIP_COL + 4 * o + c), tmp,
                                                              ALU.mult, ALU.add))
                    dst = z if o == 0 else H[:, 4 + c, first:first + n]
                    nc.vector.tensor_tensor(dst, tmp, gate, ALU.mult).then_inc(z_done, 1)

        PR = carve(Yf, [T * CT])[0]
        XT = Yf.rearrange("p (k d) -> p k d", k=6)
        ROWS4 = Hraw[:, 0:512].rearrange("p (a c) -> p a c", a=4)
        CS = Hraw[:, 512:528]
        MROW = Hraw[:, 1024:1024 + 3 * 512].rearrange("p (s n) -> p s n", s=3)
        MW = Pf[:, 0:3 * 4096].rearrange("p (s k n) -> p s k n", s=3, k=CT)
        CONST_DMAS = 16 * 2

        def rows(x):
            names = " ".join("abcd"[:len(x.shape) - 1])
            return x.rearrange(f"{names} (k c) -> ({names} k) c", c=128)

        def inputs_sp(sp):
            for dst, name in ((ident, "ident"), (ones, "ones")):
                sp.dma_start(dst[:, :], a[name]).then_inc(consts_in, 16)
            lists = (("c", "c_ctx", "norm_g"), ("mod_b",), ("hy_short_w", "hy_short_b", "hy_skip", "rw_mu"),
                     ("rw_w0", "rw_a0", "rw_k_k", "rw_k_a", "rw_r_k", "rw_ln_w", "rw_ln_b"))
            for q, names in enumerate(lists):
                at = 0
                for name in names:
                    x = a[name]
                    if name == "c_ctx":
                        src = x.rearrange("(k c) -> k c", c=128)
                    elif name == "rw_r_k":
                        src = x.rearrange("z e (k h) n -> (z e k) (h n)", h=2)
                    else:
                        src = rows(x)
                    sp.dma_start(ROWS4[at:at + src.shape[0], q, :], src).then_inc(params_in, 16)
                    at += src.shape[0]
                assert at == NROWS[q], (at, q)

            v = a["mod_w"].rearrange("l (k p) (b n) -> l b p k n", p=128, n=512)

            def block(l, b, s):
                sp.dma_start(MW[:, s, :, :], v[l][bass.ds(b, 1)].rearrange("a p k n -> (a p) k n"))\
                  .then_inc(mod_full[s], 16)

            for s in range(3):
                block(0, s, s)
            sp.dma_start(XT[:, 0:4, :], a["x"][0].rearrange("(k p) d -> p k d", p=128)).then_inc(x_in, 16)
            sp.dma_start(XT[:, 4:6, :], a["ctx"][0].rearrange("(k p) d -> p k d", p=128)).then_inc(x_in, 16)
            for l in range(2):
                with sp.Fori(1 if l == 0 else 0, 4) as i:
                    for s in range(3):
                        sp.wait_ge(mod_mm, 12 * l + 3 * i + s - 2)
                        block(l, 3 * i + s, s)

        def inputs_pe(pe):
            pe.wait_ge(consts_in, CONST_DMAS)
            pe.wait_ge(params_in, 16 * 15)
            for q, n in enumerate(NROWS):
                nc.tensor.transpose(PS[:, 4 + q, 0:n], ROWS4[0:n, q, :],
                                    ident[0:n, 0:n]).then_inc(params_T, 1)
            pe.wait_ge(c_silu, 1)
            pe.wait_ge(params_ready, 4)

            def cols(i, s):
                pe.wait_ge(mod_row, 3 * i + s + 1)
                pe.wait_ge(mod_added, 3 * i + s + 1)
                pe.sem_inc(passed, 1)
                for q in range(4):
                    last = nc.tensor.transpose(PS[:, 3 + s, 2 * q:2 * q + 2], MROW[0:2, s, 128 * q:128 * q + 128],
                                               ident[0:2, 0:2])
                last.then_inc(mod_cols, 1)

            with pe.Fori(0, 8) as i:
                for s in range(3):
                    pe.wait_ge(mod_full[s], 16 * i + 16)
                    for k in range(CT):
                        last = nc.tensor.matmul(PS[0:2, s, :], CS[:, k:k + 9:8], MW[:, s, k, :],
                                                start=k == 0, stop=k == CT - 1)
                    last.then_inc(mod_mm, 1)
                    if s:
                        cols(i, s - 1)
                cols(i, 2)
            pe.wait_ge(x_in, 32)
            for c in range(CT):
                b = 2 * (c % 3)
                pe.wait_ge(mod_added, 27)
                if c >= 3:
                    pe.wait_ge(x_evicted, c - 2)
                for k in range(6):
                    last = nc.tensor.transpose(PS[:, b + k // 3, 128 * (k % 3):128 * (k % 3) + 128],
                                               XT[:, k, 128 * c:128 * c + 128], ident[:, :])
                last.then_inc(x_T, 1)

        def inputs_act(act):
            act.wait_ge(params_ready, 1)
            nc.scalar.activation(CS, PC[:, 0:16], ACT.Silu).then_inc(c_silu, 1)
            with act.Fori(0, 8) as i:
                for s in range(3):
                    act.wait_ge(mod_mm, 3 * i + s + 1)
                    nc.scalar.activation(MROW[0:2, s, :], PS[0:2, s, :], ACT.Copy).then_inc(mod_row, 1)
            for c in range(CT):
                act.wait_ge(x_T, c + 1)
                nc.scalar.activation(as_halves(X[:, c, :]), halves(2 * (c % 3)), ACT.Copy).then_inc(x_evicted, 1)

        def inputs_dve(v):
            v.sem_inc(mod_added, 3)
            nc.vector.memset(small[:, 0:1], EPS).then_inc(consts_set, 1)
            nc.vector.memset(small[:, 1:2], -1.0).then_inc(consts_set, 1)
            nc.vector.memset(small[:, 3:4], GN_EPS).then_inc(consts_set, 1)
            for q, n in enumerate(NROWS):
                v.wait_ge(params_T, q + 1)
                nc.vector.tensor_copy(PC[:, PBASE[q]:PBASE[q] + n], PS[:, 4 + q, 0:n])\
                  .then_inc(params_ready, 1)
            v.wait_ge(params_ready, 4)
            mt = modT[:, :, :, :].rearrange("p l j w -> p (l j) w")
            with v.Fori(0, 8) as i:
                for s in range(3):
                    v.wait_ge(mod_cols, 3 * i + s + 1)
                    b = PC[:, bass.ds(PBASE[1] + 12 * i + 4 * s, 4)].unsqueeze(2).broadcast_to([128, 4, 2])
                    nc.vector.tensor_tensor(mt[:, bass.ds(12 * i + 4 * s, 4), :],
                                            PS[:, 3 + s, 0:8].rearrange("p (q w) -> p q w", w=2), b, ALU.add)\
                      .then_inc(mod_added, 1)
            v.wait_ge(mod_added, 27)
            for l in range(2):
                for w in range(2):
                    for k in range(4):
                        m = modT[:, l, 8 * (1, 2, 4, 5)[k]:8 * (1, 2, 4, 5)[k] + 8, w]
                        g = PC[:, G_COL(l, k, 0):G_COL(l, k, 0) + 8]
                        last = nc.vector.scalar_tensor_tensor(DER[:, l, k, w, :], m, 1.0 if k % 2 == 0 else 0.0, g,
                                                              ALU.add, ALU.mult)
            last.then_inc(gains_ready, 1)

        consts_set = sem("consts_set")

        def output_pe(pe, updates):
            pe.wait_ge(x_updated, updates)
            for k in range(4):
                if k >= 3:
                    pe.wait_ge(out_sb, 2 * k - 4)
                for c in range(CT):
                    last = nc.tensor.transpose(PS[:, 2 * (k % 3) + 2 + c // 4, 128 * (c % 4):128 * (c % 4) + 128],
                                               X[:, c, 128 * k:128 * k + 128], ident[:, :])
                    if c % 4 == 3:
                        last.then_inc(out_T, 1)

        def output_act(act):
            for k in range(4):
                for h in range(2):
                    act.wait_ge(out_T, 2 * k + h + 1)
                    nc.scalar.activation(Yf[:, 1024 * k + 512 * h:1024 * k + 512 * h + 512],
                                         PS[:, 2 * (k % 3) + 2 + h, :], ACT.Copy).then_inc(out_sb, 1)

        def output_sp(sp):
            for k in range(4):
                sp.wait_ge(out_sb, 2 * k + 2)
                sp.dma_start(out[0, 128 * k:128 * k + 128, :], Yf[:, 1024 * k:1024 * k + 1024]).then_inc(stored, 16)
            sp.wait_ge(stored, 64)

        Hf = lambda t, s0, s1: H[:, t, s0:s1]
        inproj = Dense("inproj", "plain", 6, 0, a["mix_w_in"][0], lambda k: H[:, k, :], P)
        outproj = Dense("outproj", "plain", 2, 6, a["mix_w_out"][0], lambda k: H[:, k, :], Y)
        gate0 = Dense("gate0", "gate", 11, 8, (a["ffn_w1"][0], a["ffn_w3"][0]), lambda k: H[:, k, :], P)
        down0 = Dense("down0", "long", 4, 19, a["ffn_w2"][0], lambda k: P[:, k, :], Y)


        def padded(t, s0, s1, shift=0):
            at = s0 + (1 if s0 < L else 2) + shift
            return Hpad[:, t, at:at + s1 - s0]

        XX = Y
        MIX = (P[:, 16:24, :], TMP[:, 0:CT * T].rearrange("p (c t) -> p c t", c=CT))
        TH, AH, GH, GH2, W2S, A2S, G2S, G2S2, EYE2, HONES, PCS, ST1 = carve(
            TMP[:, CT * T:TMPN], [T, T, L, L, 128, 128, 128, 128, 64, 128, 10, 64])
        MIXES = (5, 1, 4, 3, 2, 0)
        LORA = 23
        GR = GLORA - 128
        pads_set = sem("pads_set")
        back_in = sem("back_in")
        xx_ready = sem("xx_ready")
        mix_ready = sem("mix_ready")
        lora_hid = sem("lora_hid")
        gate_hid = sem("gate_hid")
        value = Dense("value", "plain", 2, 24, a["rw_w_rkv"][0, 2], lambda k: MIX[1][:, k, :], P[:, 8:16, :])
        key = Dense("key", "plain", 2, 26, a["rw_w_rkv"][0, 1], lambda k: MIX[0][:, k, :], P[:, 0:8, :])
        recept = Dense("recept", "plain", 2, 28, a["rw_w_rkv"][0, 0], lambda k: MIX[1][:, k, :], P[:, 16:24, :], L)

        def mixes_sp(sp):
            g1 = a["rw_g1"][0].rearrange("(k p) r -> p k r", p=128)
            parts = [(0, WR[:, 0, 0:CT, :], g1[:, :, 0:128], w_full[0]),
                     (1, WR[:, 1, 0:CT, 0:GR], g1[:, :, 128:GLORA], w_full[1])]
            for s, name in ((2, "rw_w1"), (3, "rw_a1")):
                for e in range(2):
                    parts.append((s, WR[:, s, 0:CT, 64 * e:64 * e + 64],
                                  a[name][0, e].rearrange("(k p) r -> p k r", p=128), (w_full[s], back_in)[e]))
            for s, dst, src, signal in parts:
                sp.wait_ge(slots_used, 4 * (LORA - 1) + s + 1)
                sp.dma_start(dst, src).then_inc(signal, 16)

        def mixes_pe(pe):
            jobs = ((0, MIX[0], 128, L), (1, MIX[0], GR, L), (2, MIX[1], 128, T), (3, MIX[0], 128, T))
            for s, x, m, n in jobs:
                pe.wait_ge(mix_ready, 8 * max(s, 1))
                pe.wait_ge(w_full[s], 16 * (LORA + 1))
                if s >= 2:
                    pe.wait_ge(back_in, 32)
                for k in range(CT):
                    for h0, h1, b in (((0, HALF, 0), (HALF, T, 1)) if n == T else ((0, L, 0),)):
                        last = nc.tensor.matmul(PS[0:m, 2 * s + b, 0:h1 - h0], WR[:, s, k, 0:m], x[:, k, h0:h1],
                                                start=k == 0, stop=k == CT - 1)
                last.then_inc(slots_used, 1)

        def mixes_act(act):
            u = 4 * LORA
            act.wait_ge(slots_used, u + 1)
            nc.scalar.activation(GH, PS[:, 0, 0:L], ACT.Tanh, scale=0.5).then_inc(lora_hid, 1)
            act.wait_ge(slots_used, u + 2)
            nc.scalar.activation(GH2[0:GR, :], PS[0:GR, 2, 0:L], ACT.Tanh, scale=0.5).then_inc(lora_hid, 1)
            act.wait_ge(slots_used, u + 3)
            nc.scalar.activation(as_halves(TH), halves(4), ACT.Tanh).then_inc(lora_hid, 1)
            act.wait_ge(slots_used, u + 4)
            nc.scalar.activation(as_halves(AH), halves(6), ACT.Copy).then_inc(lora_hid, 1)

        def mixes_dve(v):
            v.wait_ge(pads_set, 3)
            for t in range(CT):
                v.wait_ge(normed, NORMED_BASE[4] + t + 1)
                for s0, s1, _ in segs():
                    ins = nc.vector.tensor_tensor(XX[:, t, s0:s1], padded(t, s0, s1, -1), padded(t, s0, s1, 1), ALU.add)
                ins.then_inc(xx_ready, 1)
                v.wait_ge(xx_ready, 2 * t + 1)
                for s0, s1, _ in segs():
                    ins = nc.vector.scalar_tensor_tensor(XX[:, t, s0:s1], XX[:, t, s0:s1], 0.5, padded(t, s0, s1),
                                                         ALU.mult, ALU.subtract)
                ins.then_inc(xx_ready, 1)
            v.wait_ge(xx_ready, 2 * CT)
            used = {2: 4 * LORA + 2, 3: 4 * LORA + 3, 4: 4 * LORA + 4, 5: 4 * value.base + 8}
            for n, mu in enumerate(MIXES):
                if n in used:
                    v.wait_ge(slots_used, used[n])
                if n == 2:
                    v.wait_ge(lora_hid, 2)
                    nc.vector.tensor_scalar(GH, GH, 0.5, 0.5, ALU.mult, ALU.add).then_inc(gate_hid, 1)
                    nc.vector.tensor_scalar(GH2[0:GR, :], GH2[0:GR, :], 0.5, 0.5, ALU.mult, ALU.add)\
                      .then_inc(gate_hid, 1)
                for t in range(CT):
                    for s0, s1, _ in segs(L if mu in (0, 5) else T):
                        ins = nc.vector.scalar_tensor_tensor(MIX[n % 2][:, t, s0:s1], XX[:, t, s0:s1],
                                                             col(MU_COL + 8 * mu + t), padded(t, s0, s1),
                                                             ALU.mult, ALU.add)
                    ins.then_inc(mix_ready, 1)

        TC = 64
        NCH = T // TC
        NLAT = L // TC
        DEC0 = math.exp(-0.5)
        KRC, G, YI, RUN, ACC = carve(Hraw, [2 * T, 4 * L + 2 * C, T, T, L])
        KRC = KRC.rearrange("p (j a t) -> p j a t", j=NCH, a=2)
        GL = G[:, 0:4 * L].rearrange("p (j h a t) -> p j h a t", j=4, h=2, a=4)
        GC = G[:, 4 * L:4 * L + 2 * C].rearrange("p (j h a t) -> p j h a t", j=2, h=2, a=2)
        YI = YI.rearrange("p (x t) -> p x t", t=TC)
        BTT, KTT, VTT, XI, WI, VS, GM = carve(WRf, [T, T, T, T, T, T, 1024])
        BTT, KTT, VTT = (x.rearrange("p (j c) -> p j c", j=6) for x in (BTT, KTT, VTT))
        XI, WI = (x.rearrange("p (x t) -> p x t", t=TC) for x in (XI, WI))
        GM = GM.rearrange("p (e x a t) -> p e x a t", e=2, x=2, a=4)
        SG, SUMS, EP, EN, AA, BT, KT, KK = carve(TMP[:, 0:8 * T], [T] * 8)
        Z = Yf[:, 0:CT * L].rearrange("p (c t) -> p c t", c=CT)
        LV, YS, RHS, NSA, FIN = carve(Yf[:, CT * L:CT * T], [12 * TC, L, 128, 128, L])
        LV = LV.rearrange("p (l d t) -> p l d t", l=6, d=2)
        SPC = PCS
        PW0, PA0, PKK, PKA, PRK, PLW, PLB = 0, 2, 4, 5, 6, 8, 9

        scan_in = sem("scan_in")
        lora2_in = sem("lora2_in")
        cols_halved = sem("cols_halved")
        turn_in = sem("turn_in")
        lora_mm = sem("lora_mm")
        tanh_ready = sem("tanh_ready")
        sig_ready = sem("sig_ready")
        cs_ready = sem("cs_ready")
        decay_ready = sem("decay_ready")
        kk_raw = sem("kk_raw")
        kk_mm = sem("kk_mm")
        kk_root = sem("kk_root")
        kk_ready = sem("kk_ready")
        feat_ready = sem("feat_ready")
        gram_mm = sem("gram_mm")
        g_ready = sem("g_ready")
        tok_mm = sem("tok_mm")
        tok_ready = sem("tok_ready")
        inv_w = sem("inv_w")
        w_ready = sem("w_ready")
        inv_xy = sem("inv_xy")
        xy_ready = sem("xy_ready")
        bv_mm = sem("bv_mm")
        bv_ready = sem("bv_ready")
        rh_mm = sem("rh_mm")
        rh_ready = sem("rh_ready")
        sa_mm = sem("sa_mm")
        sa_ready = sem("sa_ready")
        st_mm = sem("st_mm")
        st_ready = sem("st_ready")
        y_mm = sem("y_mm")
        y_out = sem("y_out")
        cg_mm = sem("cg_mm")
        mean_mm = sem("mean_mm")
        centred = sem("centred")
        sq_done = sem("sq_done")
        var_mm = sem("var_mm")
        gn_root = sem("gn_root")
        z_out = sem("z_out")
        scan_step = sem("scan_step")

        def order(e):
            c, l = list(range(NLAT, NCH)), list(range(NLAT))
            return c + l if e == 0 else c[::-1] + l[::-1]

        def gram(j, h, p, which):
            r = slice(64 * p, 64 * p + 64)
            return GL[r, j, h, which, :] if j < 4 else GC[r, j - 4, h, which // 2, :]

        def scan_sp(sp):
            sp.wait_ge(slots_used, 4 * recept.base + 8)
            for dst, name in ((GM, "grammask"), (LV, "levelmask"), (EYE2, "eye2"), (RUN, "run"), (HONES, "headones")):
                if name == "grammask":
                    src = a[name].rearrange("p e (x a t) -> p e x a t", x=2, a=4)
                else:
                    src = a[name]
                sp.dma_start(dst, src).then_inc(scan_in, 16)
            with sp.Fori(0, CT) as i:
                sp.wait_ge(z_out, i + 1)
                for dst, src in ((W2S, a["rw_w2"][0].rearrange("e r (c d) -> c (e r) d", d=128)),
                                 (A2S, a["rw_a2"][0].rearrange("e r (c d) -> c (e r) d", d=128)),
                                 (G2S, a["rw_g2"][0, 0:128, :].rearrange("r (c d) -> c r d", d=128)),
                                 (G2S2[0:GR, :], a["rw_g2"][0, 128:GLORA, :].rearrange("r (c d) -> c r d", d=128))):
                    sp.dma_start(dst, src[bass.ds(i, 1)].rearrange("a r d -> (a r) d")).then_inc(lora2_in, 16)

        def scan_pool(pool):
            pool.wait_ge(cols_halved, 1)
            pool.wait_ge(recept.unit_free, recept.done)
            pool.wait_ge(slots_used, 4 * recept.base + 8)
            pc = PC[:, PBASE[3]:PBASE[3] + 80].rearrange("p (g c) -> p g c", c=8)
            with pool.Fori(0, CT) as i:
                pool.wait_ge(z_out, i + 1)
                nc.gpsimd.tensor_copy(PCS.unsqueeze(2), pc[:, :, bass.ds(i, 1)]).then_inc(turn_in, 1)
                nc.gpsimd.tensor_copy(VS, P[:, bass.ds(8 + i, 1), :].rearrange("p a t -> p (a t)")).then_inc(turn_in, 1)
                for e in range(2):
                    u = 2 * i + e
                    for k, x in enumerate((SG, AA)):
                        pool.wait_ge(tanh_ready, 2 * u + k + 1)
                        pool.sem_inc(passed, 1)
                        nc.gpsimd.tensor_scalar(x, x, 0.5, 0.5, ALU.mult, ALU.add).then_inc(sig_ready, 1)

        def scan_pe(pe):
            def cover(e, i):
                u = 2 * i + e
                pe.wait_ge(lora2_in, 64 * i + 64)
                if e == 0:
                    pe.wait_ge(z_out, i + 1)
                else:
                    pe.wait_ge(y_out, 2 * i + 1)
                r = slice(64 * e, 64 * e + 64)
                pe.sem_inc(passed, 1)
                for b, w, x in ((0, W2S, TH), (2, A2S, AH)):
                    for h in range(2):
                        last = nc.tensor.matmul(PS[:, b + h, 0:HALF], w[r, :], x[r, HALF * h:HALF * h + HALF],
                                                start=True, stop=True)
                    last.then_inc(lora_mm, 1)
                if e == 0:
                    pe.wait_ge(kk_raw, 2 * i + 2)
                    pe.sem_inc(passed, 1)
                    for h in range(2):
                        last = nc.tensor.matmul(PS[:, 4 + h, 0:HALF], HONES, BT[:, HALF * h:HALF * h + HALF],
                                                start=True, stop=True)
                    last.then_inc(kk_mm, 1)

                def tokens(n, src):
                    pe.wait_ge(tok_ready, 5 * i + n + 1)
                    for k in range(6):
                        last = nc.tensor.transpose(PS[:, 6 + k // 3, 128 * (k % 3):128 * (k % 3) + 128],
                                                   src[:, 128 * k:128 * k + 128], ident[:, :])
                    last.then_inc(tok_mm, 1)
                if e == 0:
                    pe.wait_ge(turn_in, 2 * i + 2)
                    tokens(0, VS)
                pe.wait_ge(feat_ready, u + 1)
                pe.sem_inc(passed, 1)
                for q in range(3):
                    for h in range(2):
                        hr = slice(64 * h, 64 * h + 64)
                        for j in (2 * q, 2 * q + 1):
                            for p in range(2):
                                ch = 2 * j + p
                                pr = slice(64 * p, 64 * p + 64)
                                for w, x in ((0, BT), (1, KT)):
                                    n = 128 if j < 4 else 64
                                    at = 2 * n * (j % 2) + n * w
                                    last = nc.tensor.matmul(PS[pr, q + 3 * h, at:at + n], x[hr, 64 * ch:64 * ch + 64],
                                                            KRC[hr, ch, 0:n // 64, :], start=True, stop=True)
                        last.then_inc(gram_mm, 1)
                tokens(1 + 2 * e, BT)
                tokens(2 + 2 * e, KT)

                def all_products(bank, lhs, rhs):
                    for j in range(6):
                        for h in range(2):
                            x = 2 * j + h
                            for p in range(2):
                                pr = slice(64 * p, 64 * p + 64)
                                last = nc.tensor.matmul(
                                    PS[pr, bank + x // 6, 64 * (x % 6):64 * (x % 6) + 64],
                                    lhs(j, h, p, x, pr), rhs(j, h, p, x, pr), start=True, stop=True)
                    return last
                a_t = lambda j, h, p, x, pr: gram(j, h, p, 0)
                xi = lambda j, h, p, x, pr: XI[pr, x, :]
                yi = lambda j, h, p, x, pr: YI[pr, x, :]
                wi = lambda j, h, p, x, pr: WI[pr, x, :]
                pe.wait_ge(g_ready, 6 * u + 6)
                pe.sem_inc(passed, 1)
                all_products(0, a_t, lambda j, h, p, x, pr: EYE2[pr, :]).then_inc(inv_w, 1)
                for l in range(1, 6):
                    pe.wait_ge(xy_ready, 6 * u + l)
                    pe.sem_inc(passed, 1)
                    all_products(0, a_t, xi).then_inc(inv_w, 1)
                    pe.wait_ge(w_ready, 6 * u + l + 1)
                    pe.sem_inc(passed, 1)
                    if l < 5:
                        all_products(2, yi, wi)
                    all_products(4, wi, yi).then_inc(inv_xy, 1)
                pe.wait_ge(tok_ready, 5 * i + 2 * e + 4)
                pe.sem_inc(passed, 1)
                all_products(2, lambda j, h, p, x, pr: gram(j, h, p, 2),
                             lambda j, h, p, x, pr: VTT[pr, j, 64 * h:64 * h + 64]).then_inc(bv_mm, 1)
                pe.wait_ge(bv_ready, u + 1)
                for n, ch in enumerate(order(e)):
                    j, p = ch // 2, ch % 2
                    pr = slice(64 * p, 64 * p + 64)
                    latent = ch < NLAT
                    if n == 0:
                        pe.wait_ge(xy_ready, 6 * u + 6)
                    pe.wait_ge(st_ready, 13 * u + n + 1)
                    pe.sem_inc(passed, 1)
                    for h in range(2):
                        hr = slice(64 * h, 64 * h + 64)
                        last = nc.tensor.matmul(PS[pr, 6 + h, 0:64], KRC[hr, ch, 0, :], ST1[hr, :],
                                                start=True, stop=True)
                    last.then_inc(rh_mm, 1)
                    if latent:
                        for h in range(2):
                            hr = slice(64 * h, 64 * h + 64)
                            nc.tensor.matmul(PS[hr, 1, 64 * ch:64 * ch + 64], ST1[hr, :], KRC[hr, ch, 1, :],
                                             start=True, stop=True)
                    pe.wait_ge(rh_ready, 12 * u + n + 1)
                    pe.sem_inc(passed, 1)
                    for h in range(2):
                        hv = slice(64 * h, 64 * h + 64)
                        last = nc.tensor.matmul(PS[pr, 5, hv], YI[pr, 2 * j + h, :], RHS[pr, hv], start=True, stop=True)
                    last.then_inc(sa_mm, 1)
                    pe.wait_ge(sa_ready, 12 * u + n + 1)
                    pe.sem_inc(passed, 1)
                    for h in range(2):
                        hr = slice(64 * h, 64 * h + 64)
                        nc.tensor.matmul(PS[hr, 0, 0:64], BTT[pr, j, hr], NSA[pr, hr], start=True, stop=False)
                        last = nc.tensor.matmul(PS[hr, 0, 0:64], KTT[pr, j, hr], VTT[pr, j, hr], start=False, stop=True)
                    last.then_inc(st_mm, 1)
                    if latent:
                        for h in range(2):
                            hr = slice(64 * h, 64 * h + 64)
                            nc.tensor.matmul(PS[hr, 2, 64 * ch:64 * ch + 64], VTT[pr, j, hr], gram(j, h, p, 3),
                                             start=True, stop=False)
                            last = nc.tensor.matmul(PS[hr, 2, 64 * ch:64 * ch + 64], NSA[pr, hr], gram(j, h, p, 1),
                                                    start=False, stop=True)
                        if n == NCH - 1:
                            last.then_inc(y_mm, 1)

            with pe.Fori(0, CT) as i:
                for e in range(2):
                    cover(e, i)
                pe.wait_ge(y_out, 2 * i + 2)
                pe.sem_inc(passed, 1)
                nc.tensor.matmul(PS[:, 2, 0:L], HONES, ACC, start=True, stop=True)
                nc.tensor.matmul(PS[:, 3, 0:L], G2S, GH, start=True, stop=False)
                nc.tensor.matmul(PS[:, 3, 0:L], G2S2[0:GR, :], GH2[0:GR, :], start=False, stop=True).then_inc(cg_mm, 1)
                nc.tensor.matmul(PS[:, 4, 0:L], HONES, YS, start=True, stop=True).then_inc(mean_mm, 1)
                pe.wait_ge(sq_done, i + 1)
                pe.sem_inc(passed, 1)
                nc.tensor.matmul(PS[:, 5, 0:L], HONES, FIN, start=True, stop=True).then_inc(var_mm, 1)

        def scan_act(act):
            def evict_tokens(i, n, dst):
                act.wait_ge(tok_mm, 5 * i + n + 1)
                nc.scalar.activation(dst[:, :, :].rearrange("p (g k) c -> p g k c", g=2),
                                     halves(6).rearrange("p g (k c) -> p g k c", k=3), ACT.Copy).then_inc(tok_ready, 1)
            act.sem_inc(tok_ready, 1)
            with act.Fori(0, CT) as i:
                for e in range(2):
                    u = 2 * i + e
                    if e == 0:
                        act.wait_ge(turn_in, 2 * i + 2)
                        act.wait_ge(z_out, i + 1)
                        act.sem_inc(passed, 1)
                        nc.scalar.activation(KK, P[:, bass.ds(i, 1), :].rearrange("p a t -> p (a t)"), ACT.Copy,
                                             scale=PCS[:, PKK:PKK + 1]).then_inc(kk_raw, 1)
                        act.wait_ge(kk_raw, 2 * i + 1)
                        nc.scalar.activation(BT, KK, ACT.Square).then_inc(kk_raw, 1)
                        act.wait_ge(kk_mm, i + 1)
                        nc.scalar.activation(as_halves(KT), halves(4), ACT.Sqrt).then_inc(kk_root, 1)
                        evict_tokens(i, 0, VTT)
                    for k, (x, w) in enumerate(((SG, PW0), (AA, PA0))):
                        act.wait_ge(lora_mm, 2 * u + k + 1)
                        nc.scalar.activation(as_halves(x), halves(2 * k), ACT.Tanh, scale=0.5,
                                             bias=PCS[:, w + e:w + e + 1]).then_inc(tanh_ready, 1)
                    act.wait_ge(cs_ready, u + 1)
                    nc.scalar.activation(EP, SUMS, ACT.Exp, scale=-DEC0)
                    nc.scalar.activation(EN, SUMS, ACT.Exp, scale=DEC0).then_inc(decay_ready, 1)
                    evict_tokens(i, 1 + 2 * e, BTT)
                    evict_tokens(i, 2 + 2 * e, KTT)
                    act.wait_ge(bv_mm, u + 1)
                    nc.scalar.activation(WI[:, :, :].rearrange("p (b x) t -> p b x t", b=2),
                                         PS[:, 2:4, 0:HALF].rearrange("p b (x t) -> p b x t", t=TC), ACT.Copy)\
                      .then_inc(bv_ready, 1)
                    for n, ch in enumerate(order(e)):
                        p = ch % 2
                        pr = slice(64 * p, 64 * p + 64)
                        act.wait_ge(sa_mm, 12 * u + n + 1)
                        nc.scalar.activation(NSA[pr, :], PS[pr, 5, 0:128], ACT.Copy, scale=-1.0).then_inc(sa_ready, 1)
                act.wait_ge(centred, i + 1)
                nc.scalar.activation(FIN, YS, ACT.Square).then_inc(sq_done, 1)
                act.wait_ge(var_mm, i + 1)
                nc.scalar.activation(FIN, PS[:, 5, 0:L], ACT.Sqrt, scale=1.0 / CH, bias=small[:, 3:4]).then_inc(gn_root, 1)

        SCAN_LINKS = 3 + 2 * 4 + 1 + 2 * NCH + 2 + 5

        def scan_dve(v):
            v.sem_inc(z_out, 1)
            nc.vector.tensor_scalar(PC[:, W0_COL:W0_COL + 32], PC[:, W0_COL:W0_COL + 32], 0.5, None, ALU.mult)\
              .then_inc(cols_halved, 1)
            chain = Chain(v, scan_step, SCAN_LINKS)
            v.wait_ge(scan_in, 16 * 5)
            v.wait_ge(recept.unit_free, recept.done)

            def turn(e, i):
                u = 2 * i + e
                kdyn = P[:, bass.ds(i, 1), :].rearrange("p a t -> p (a t)")
                rdyn = P[:, bass.ds(16 + i, 1), 0:L].rearrange("p a t -> p (a t)")
                chunks = lambda x: x.rearrange("p (j t) -> p j t", t=TC)
                v.wait_ge(sig_ready, 2 * u + 1)
                nc.vector.memset(ST1, 0.0).then_inc(st_ready, 1)
                if e == 0:
                    nc.vector.tensor_tensor_scan(SUMS, RUN, SG, 0.0, ALU.mult, ALU.add).then_inc(cs_ready, 1)
                else:
                    nc.vector.tensor_tensor_scan(SUMS[:, ::-1], RUN, SG[:, ::-1], 0.0, ALU.mult, ALU.add)\
                      .then_inc(cs_ready, 1)
                if e == 0:
                    v.wait_ge(kk_root, i + 1)
                    chain.link(nc.vector.tensor_scalar(KT, KT, 1e-12, None, ALU.max))
                    chain.link(nc.vector.reciprocal(KT, KT))
                    chain.link(nc.vector.tensor_tensor(KK, KK, KT, ALU.mult))
                v.wait_ge(decay_ready, u + 1)
                v.wait_ge(sig_ready, 2 * u + 2)
                if e == 1:
                    v.wait_ge(tok_mm, 5 * i + 3)
                chain.link(nc.vector.tensor_tensor(BT, KK, AA, ALU.mult))
                nc.vector.tensor_tensor(BT, BT, EN, ALU.mult)
                kin = KRC[:, :, 0, :]
                kc, ec = chunks(KK), chunks(EP)
                if e == 0:
                    nc.vector.tensor_tensor(kin[:, :, 1:TC], kc[:, :, 1:TC], ec[:, :, 0:TC - 1], ALU.mult)
                    nc.vector.tensor_copy(kin[:, :, 0:1], kc[:, :, 0:1])
                else:
                    nc.vector.tensor_tensor(kin[:, :, 0:TC - 1], kc[:, :, 0:TC - 1], ec[:, :, 1:TC], ALU.mult)
                    nc.vector.tensor_copy(kin[:, :, TC - 1:TC], kc[:, :, TC - 1:TC])
                nc.vector.tensor_tensor(KRC[:, 0:NLAT, 1, :], chunks(rdyn), chunks(EP[:, 0:L]), ALU.mult)
                chain.link(nc.vector.tensor_scalar(AA, AA, 1.0, PCS[:, PKA:PKA + 1], ALU.subtract, ALU.mult))
                chain.link(nc.vector.scalar_tensor_tensor(SUMS, AA, 1.0, kdyn, ALU.add, ALU.mult))
                nc.vector.tensor_tensor(KT, SUMS, EN, ALU.mult).then_inc(feat_ready, 1)
                if e == 0:
                    nc.vector.tensor_scalar(ACC, SUMS[:, 0:L], PCS[:, PRK:PRK + 1], None, ALU.mult)
                else:
                    chain.link(nc.vector.scalar_tensor_tensor(ACC, SUMS[:, 0:L], PCS[:, PRK + 1:PRK + 2], ACC,
                                                              ALU.mult, ALU.add))
                    nc.vector.tensor_tensor(ACC, ACC, rdyn, ALU.mult)
                for q in range(3):
                    for h in range(2):
                        v.wait_ge(gram_mm, 6 * u + 2 * q + h + 1)
                        if q < 2:
                            nc.vector.tensor_tensor(GL[:, 2 * q:2 * q + 2, h, :, :], GM[:, e, :, :, :],
                                                    PS[:, q + 3 * h, :].rearrange("p (j a t) -> p j a t", j=2, a=4),
                                                    ALU.mult).then_inc(g_ready, 1)
                        else:
                            nc.vector.tensor_tensor(
                                GC[:, :, h, :, :], GM[:, e, 0:1, 0:1, :].broadcast_to([128, 2, 2, TC]),
                                PS[:, q + 3 * h, 0:256].rearrange("p (j a t) -> p j a t", j=2, a=2),
                                ALU.mult).then_inc(g_ready, 1)
                v.wait_ge(g_ready, 6 * u + 6)
                psw, psx, psy = (PS[:, b:b + 2, 0:HALF].rearrange("p b (x t) -> p b x t", t=TC) for b in (0, 2, 4))
                split = lambda x: x[:, :, :].rearrange("p (b x) t -> p b x t", b=2)

                def mask(l, d, n=6):
                    return LV[:, l, d:d + 1, :].broadcast_to([128, n, TC])
                eye = EYE2.unsqueeze(1).broadcast_to([128, 12, TC])
                gl_a = GL[:, :, :, 0, :]
                gc_a = GC[:, :, :, 0, :]
                nc.vector.tensor_tensor(YI[:, 0:8, :].rearrange("p (j h) t -> p j h t", h=2), gl_a,
                                        LV[:, 0, 1 - e:2 - e, :].unsqueeze(1).broadcast_to([128, 4, 2, TC]), ALU.mult)
                chain.link(nc.vector.tensor_tensor(
                    YI[:, 8:12, :].rearrange("p (j h) t -> p j h t", h=2), gc_a,
                    LV[:, 0, 1 - e:2 - e, :].unsqueeze(1).broadcast_to([128, 2, 2, TC]), ALU.mult))
                nc.vector.tensor_tensor(YI[:, :, :], eye, YI[:, :, :], ALU.subtract)
                v.wait_ge(inv_w, 6 * u + 1)
                for b in range(2):
                    ins = nc.vector.tensor_tensor(XI[:, 6 * b:6 * b + 6, :], psw[:, b], mask(0, e), ALU.mult)
                ins.then_inc(w_ready, 1)
                v.wait_ge(w_ready, 6 * u + 1)
                nc.vector.tensor_tensor(XI[:, :, :], eye, XI[:, :, :], ALU.subtract).then_inc(xy_ready, 1)
                for l in range(1, 6):
                    v.wait_ge(inv_w, 6 * u + l + 1)
                    for b in range(2):
                        ins = nc.vector.tensor_tensor(WI[:, 6 * b:6 * b + 6, :], psw[:, b], mask(l, e), ALU.mult)
                    ins.then_inc(w_ready, 1)
                    v.wait_ge(inv_xy, 5 * u + l)
                    v.wait_ge(xy_ready, 6 * u + l)
                    if l < 5:
                        nc.vector.tensor_tensor(split(XI), split(XI), psx, ALU.subtract)
                    nc.vector.tensor_tensor(split(YI), split(YI), psy, ALU.subtract).then_inc(xy_ready, 1)
                for n, ch in enumerate(order(e)):
                    end = 64 * ch + (63 if e == 0 else 0)
                    pr = slice(64 * (ch % 2), 64 * (ch % 2) + 64)
                    j = ch // 2
                    v.wait_ge(rh_mm, 12 * u + n + 1)
                    v.wait_ge(bv_ready, u + 1)
                    nc.vector.tensor_tensor(RHS[pr, :].rearrange("p (h t) -> p h t", h=2), WI[pr, 2 * j:2 * j + 2, :],
                                            PS[pr, 6:8, 0:64], ALU.add).then_inc(rh_ready, 1)
                    v.wait_ge(st_mm, 12 * u + n + 1)
                    v.wait_ge(st_ready, 13 * u + n + 1)
                    chain.link(nc.vector.tensor_tensor(ST1, ST1, PS[:, 0, 0:64], ALU.add))
                    nc.vector.tensor_scalar(ST1, ST1, EP[:, end:end + 1], None, ALU.mult).then_inc(st_ready, 1)
                v.wait_ge(y_mm, u + 1)
                if e == 0:
                    chain.link(nc.vector.tensor_scalar(YS, PS[:, 1, :], 1.0, None, ALU.mult))
                else:
                    chain.link(nc.vector.tensor_tensor(YS, YS, PS[:, 1, :], ALU.add))
                nc.vector.tensor_tensor(YS, YS, PS[:, 2, :], ALU.add).then_inc(y_out, 1)

            with v.Fori(0, CT) as i:
                chain.start(i)
                for e in range(2):
                    turn(e, i)
                vdyn = P[:, bass.ds(8 + i, 1), 0:L].rearrange("p a t -> p (a t)")
                v.wait_ge(mean_mm, i + 1)
                nc.vector.scalar_tensor_tensor(YS, PS[:, 4, :], -1.0 / CH, YS, ALU.mult, ALU.add).then_inc(centred, 1)
                v.wait_ge(gn_root, i + 1)
                chain.link(nc.vector.reciprocal(FIN, FIN))
                chain.link(nc.vector.tensor_tensor(YS, YS, FIN, ALU.mult))
                chain.link(nc.vector.tensor_scalar(YS, YS, PCS[:, PLW:PLW + 1], PCS[:, PLB:PLB + 1], ALU.mult, ALU.add))
                chain.link(nc.vector.tensor_tensor(FIN, PS[:, 2, :], vdyn, ALU.mult))
                chain.link(nc.vector.tensor_tensor(YS, YS, FIN, ALU.add))
                nc.vector.tensor_tensor(Z[:, bass.ds(i, 1), :].rearrange("p a t -> p (a t)"), YS, PS[:, 3, :], ALU.mult)\
                  .then_inc(z_out, 1)
                chain.end()
        mixout = Dense("mixout", "plain", 2, 30, a["rw_w_o"][0], lambda k: Z[:, k, :], H, L)
        gate1 = Dense("gate1", "gate", 11, 32, (a["ffn_w1"][1], a["ffn_w3"][1]), lambda k: Y[:, k, 0:L], P, L)
        down1 = Dense("down1", "long", 4, 43, a["ffn_w2"][1], lambda k: P[:, k, 0:L], H, L)
        Yt = lambda t: Y[:, t, :]
        Xt = lambda t: X[:, t, :]
        Xl = lambda t: X[:, t, 0:L]
        Hl = lambda t: H[:, t, 0:L]

        block = ctx.enter_context(nc.Block())

        @block.sync
        def _(sp):
            inputs_sp(sp)
            dense_load(sp, inproj, first=True)
            sp.wait_ge(x_evicted, 8)
            for dst, src in ((RPL[0:NH * ND, :], a["na_rpb"].rearrange("a h d m -> (a h d) m")),
                             (PICK[0:64, :], a["pick"]), (WINDOW, a["window"])):
                sp.dma_start(dst, src).then_inc(bias_in, 16)
            hyena_sp(sp)
            dense_load(sp, outproj)
            dense_load(sp, gate0)
            dense_load(sp, down0)
            mixes_sp(sp)
            dense_load(sp, value)
            dense_load(sp, key)
            dense_load(sp, recept)
            scan_sp(sp)
            sp.wait_ge(z_out, CT + 1)
            dense_load(sp, mixout)
            dense_load(sp, gate1)
            dense_load(sp, down1)
            output_sp(sp)

        @block.tensor
        def _(pe):
            inputs_pe(pe)
            norm_pe(pe, 0, T, lambda e: None)
            pe.wait_ge(normed, 8)
            dense_pe(pe, inproj)
            bias_pe(pe)
            attn_pe(pe)
            mlp_pe(pe)
            pe.wait_ge(attn_out, 2 + NH)
            pe.wait_ge(conv3_done, 12)
            hyena_pe(pe)
            pe.wait_ge(z_done, 16)
            dense_pe(pe, outproj)
            norm_pe(pe, 1, T, lambda e: None)
            norm_pe(pe, 2, T, lambda e: None)
            pe.wait_ge(normed, 16)
            dense_pe(pe, gate0)
            pe.wait_ge(gate0.unit_free, gate0.done)
            dense_pe(pe, down0)
            norm_pe(pe, 3, T, lambda e: None)
            norm_pe(pe, 4, T, lambda e: None)
            mixes_pe(pe)
            pe.wait_ge(lora_hid, 4)
            pe.wait_ge(mix_ready, 32)
            dense_pe(pe, value)
            pe.wait_ge(mix_ready, 40)
            pe.wait_ge(value.unit_free, value.done)
            dense_pe(pe, key)
            pe.wait_ge(mix_ready, 48)
            pe.wait_ge(key.unit_free, key.done)
            dense_pe(pe, recept)
            pe.wait_ge(recept.unit_free, recept.done)
            pe.wait_ge(scan_in, 80)
            pe.wait_ge(gate_hid, 2)
            scan_pe(pe)
            pe.wait_ge(z_out, CT + 1)
            dense_pe(pe, mixout)
            norm_pe(pe, 5, L, lambda e: None)
            norm_pe(pe, 6, L, lambda e: None)
            pe.wait_ge(normed, 32)
            dense_pe(pe, gate1)
            pe.wait_ge(gate1.unit_free, gate1.done)
            dense_pe(pe, down1)
            norm_pe(pe, 7, L, lambda e: None)
            output_pe(pe, 32)

        @block.scalar
        def _(act):
            inputs_act(act)
            act.wait_ge(consts_set, 3)
            norm_squares_act(act, 0, lambda t: X[:, t, :], T, lambda e, t: e.wait_ge(x_evicted, t + 1))
            act.wait_ge(gains_ready, 1)
            norm_shift_act(act, 0, T, 0, 0, Hf)
            dense_evict_act(act, inproj)
            attn_act(act)
            mlp_act(act)
            hyena_act(act)
            dense_evict_act(act, outproj)
            norm_squares_act(act, 1, lambda t: Y[:, t, :], T, lambda e, t: e.wait_ge(outproj.unit_free, outproj.done))
            norm_squares_act(act, 2, lambda t: X[:, t, :], T, lambda e, t: e.wait_ge(x_updated, t + 1))
            norm_shift_act(act, 2, T, 0, 2, Hf)
            dense_evict_act(act, gate0)
            dense_evict_act(act, down0)
            norm_squares_act(act, 3, lambda t: Y[:, t, :], T, lambda e, t: e.wait_ge(down0.unit_free, down0.done))
            norm_squares_act(act, 4, Xt, T, lambda e, t: e.wait_ge(x_updated, 8 + t + 1))
            norm_shift_act(act, 4, T, 1, 0, padded)
            mixes_act(act)
            dense_evict_act(act, value)
            dense_evict_act(act, key)
            dense_evict_act(act, recept)
            scan_act(act)
            dense_evict_act(act, mixout)
            norm_squares_act(act, 5, Hl, L, lambda e, t: e.wait_ge(mixout.unit_free, mixout.done))
            norm_squares_act(act, 6, Xl, L, lambda e, t: e.wait_ge(x_updated, 16 + t + 1))
            norm_shift_act(act, 6, L, 1, 2, lambda t, s0, s1: Y[:, t, s0:s1])
            dense_evict_act(act, gate1)
            dense_evict_act(act, down1)
            norm_squares_act(act, 7, Hl, L, lambda e, t: e.wait_ge(down1.unit_free, down1.done))
            output_act(act)

        @block.gpsimd
        def _(pool):
            attn_pool(pool)
            pool.wait_ge(slots_used, 4 * down0.base)
            for at in (0, L + 1, T + 2):
                nc.gpsimd.memset(Hpad[:, :, at:at + 1], 0.0).then_inc(pads_set, 1)
            scan_pool(pool)

        @block.vector
        def _(v):
            chain = Chain(v, dve_step)
            inputs_dve(v)
            v.wait_ge(gains_ready, 1)
            v.wait_ge(x_evicted, 8)
            norm_scale_dve(v, 0, lambda t: X[:, t, :], T)
            bias_dve(v)
            attn_dve(v)
            conv3_dve(v)
            mlp_dve(v, chain)
            hyena_dve(v, chain)
            norm_scale_dve(v, 1, lambda t: Y[:, t, :], T, residual=(0, 1))
            norm_scale_dve(v, 2, lambda t: X[:, t, :], T)
            gate_evict_dve(v, gate0, 0)
            norm_scale_dve(v, 3, Yt, T, residual=(0, 3))
            norm_scale_dve(v, 4, Xt, T)
            mixes_dve(v)
            scan_dve(v)
            norm_scale_dve(v, 5, Hl, L, residual=(1, 1))
            norm_scale_dve(v, 6, Xl, L)
            gate_evict_dve(v, gate1, 22)
            norm_scale_dve(v, 7, Hl, L, residual=(1, 3))


_INS = ["x", "c", "ctx", "c_ctx", "mod_w", "mod_b", "norm_g", "ffn_w1", "ffn_w3", "ffn_w2", "mix_w_in", "mix_w_out",
        "na_rpb", "hy_short_w", "hy_short_b", "hy_pos_w1", "hy_pos_b1", "hy_pos_w2", "hy_pos_b2", "hy_pos_w3",
        "hy_sin_freq", "hy_skip", "rw_mu", "rw_w_rkv", "rw_w_o", "rw_w0", "rw_w1", "rw_w2", "rw_a0", "rw_a1",
        "rw_a2", "rw_g1", "rw_g2", "rw_k_k", "rw_k_a", "rw_r_k", "rw_ln_w", "rw_ln_b"]


def kernel(**inputs):
    import numpy as _np
    import concourse.bacc as _bacc
    from concourse import mybir as _mybir
    from concourse.bass_utils import run_bass_kernel_spmd as _run

    nc = _bacc.Bacc("TRN2", target_bir_lowering=False, num_devices=1)
    given = {name: _np.ascontiguousarray(inputs[name]) for name in _INS}
    given.update(shape_constants())
    arrays, aps = {}, {}
    for name, x in given.items():
        arrays[f"in_{name}_dram"] = x
        aps[name] = nc.dram_tensor(f"in_{name}_dram", x.shape, _mybir.dt.from_np(x.dtype), kind="ExternalInput").ap()
    out = nc.dram_tensor("out_0_dram", (1, L, D), F32, kind="ExternalOutput").ap()
    hybrid_dit_kernel(nc, aps, out)
    r = _run(nc, [arrays], core_ids=[0])
    return r.results[0]["out_0_dram"]
```

```python
import concourse.bass as bass
from concourse import mybir
from contextlib import ExitStack
import numpy as np
import math

F32 = mybir.dt.float32
ALU = mybir.AluOpType
ACT = mybir.ActivationFunctionType
AX_X = mybir.AxisListType.X

D = 1024
L = 512
C = 256
T = L + C
CT = D // 128
F = 2816
FT = F // 128
HALF = T // 2
GRID = 64
ROWS = L // GRID
WIN = 16
NH = 8
HW = 512
ORD = 2
EMB = 33
HID = 64
RH = 16
CH = 64
DLORA = 64
GLORA = 160
EPS = 1e-6
GN_EPS = 64e-5
PI = math.pi
SLOTS = 4
SLOT_K = 11
HP = T + 3


def shape_constants():
    f4 = np.float32
    t = {}
    i = np.arange(128)
    t["ident"] = np.eye(128, dtype=f4)
    t["ones"] = np.full((128, 128), 1.0 / D, f4)
    t["headones"] = (i[:, None] // 64 == i[None, :] // 64).astype(f4)
    u = np.zeros((64, 3 * GRID - 1), f4)
    for m in range(2 * WIN - 1):
        for r in range(2):
            u[32 * r + m, GRID * (r + 1) + WIN - 2 - m] = 1.0
    t["pick"] = u
    col = np.arange(GRID)
    start = np.clip(col - WIN // 2, 0, GRID - WIN)
    inside = (col[None, :] >= start[:, None]) & (col[None, :] < start[:, None] + WIN)
    t["window"] = np.tile(np.where(inside, 0.0, -1e30), (2, 1)).astype(f4)
    for n in (L, C):
        th = np.pi * np.outer(np.arange(n), 2 * np.arange(n) + 1) / (2 * n)
        m = np.stack([np.cos(th), np.sin(th), np.cos(th).T / n, np.sin(th).T / n])
        t[f"dft{n}"] = np.ascontiguousarray(
            m.reshape(4, n // 128, 128, n).transpose(2, 0, 1, 3)).astype(f4)
    bands = (EMB - 1) // 2
    feats, cols = [], []
    for n in (L, C):
        pos = np.arange(n, dtype=f4)
        tt = np.linspace(0.0, 1.0, n, dtype=f4)
        ang = f4(2.0 * math.pi / n) * pos[:, None] * np.linspace(1e-4, bands - 1, bands, dtype=f4)[None, :]
        feats.append(np.concatenate([tt[:, None], np.cos(ang), -np.sin(ang)], -1).T)
        c = -tt.reshape(n // 128, 128).T
        back = c.copy()
        back[0, 0] = -1e4
        cols += [c, back]
    t["feats"] = np.concatenate(feats, 1).astype(f4)
    t["times"] = np.concatenate(cols, 1).astype(f4)
    lo, hi = math.log(1e-2) / 1.5, math.log(1e-2) / 0.3
    t["deltas"] = np.tile(np.abs(np.linspace(lo, hi, HW, dtype=f4))[None], (128, 1))
    s, q = np.arange(64)[:, None], np.arange(64)[None, :]
    gram = np.stack([s < q, s <= q, s > q, s >= q], 1).reshape(64, 2, 2, 64)
    t["grammask"] = np.tile(gram, (2, 1, 1, 1)).astype(f4)
    lev = []
    for m in (16, 32):
        same = (s // (2 * m)) == (q // (2 * m))
        later = same & (s % (2 * m) >= m) & (q % (2 * m) < m)
        lev.append([later, later.T])
    lev = np.array(lev).astype(f4)
    t["levelmask"] = np.ascontiguousarray(np.tile(lev.transpose(2, 0, 1, 3), (2, 1, 1, 1)))
    run = np.ones((128, T), f4)
    run[:, ::64] = 0.0
    t["run"] = run
    return t


def hybrid_dit_kernel(nc, a, out):
    ctx = ExitStack()
    with ctx:
        def sb(name, shape, dt=F32):
            return ctx.enter_context(nc.sbuf_tensor(name, shape, dt))

        def sem(name):
            return ctx.enter_context(nc.semaphore(name))

        PS = ctx.enter_context(nc.psum_tensor("PS", [128, 8, 512], F32))

        NROWS = (80, 96, 104, 80)
        PBASE = (0, 80, 176, 280)

        X = sb("X", [128, CT, T])
        Hraw = sb("Hraw", [128, CT * HP])
        H = Hraw[:, 0:CT * T].rearrange("p (c t) -> p c t", c=CT)
        Hpad = Hraw[:, :].rearrange("p (c t) -> p c t", c=CT)
        Y = sb("Y", [128, CT, T])
        Yf = Y[:, :, :].rearrange("p c t -> p (c t)")
        P = sb("P", [128, 24, T])
        Pf = P[:, :, :].rearrange("p c t -> p (c t)")
        WR = sb("WR", [128, SLOTS, SLOT_K, 128])
        WRf = WR[:, :, :, :].rearrange("p s k m -> p (s k m)")
        TMPN = 9624
        TMP = sb("TMP", [128, TMPN])
        ident = sb("ident", [128, 128])
        ones = sb("ones", [128, 128])
        PC = sb("PC", [128, sum(NROWS)])
        modT = sb("modT", [128, 2, 48, 2])
        DER = sb("DER", [128, 2, 4, 2, 8])
        small = sb("small", [128, 64])

        def carve(base, sizes):
            views, at = [], 0
            for n in sizes:
                views.append(base[:, at:at + n])
                at += n
            assert at <= base.shape[1], (at, base.shape)
            return views

        def col(k):
            return PC[:, k:k + 1]

        G_COL = lambda l, k, t: 16 + (l * 4 + k) * 8 + t
        SW_COL, SB_COL, SKIP_COL, MU_COL = (PBASE[2] + x for x in (0, 36, 48, 56))
        W0_COL, A0_COL, KK_COL, KA_COL, RK_COL, LNW_COL, LNB_COL = (PBASE[3] + x for x in (0, 16, 32, 40, 48, 64, 72))

        def halves(bank, n=T):
            if n == T:
                return PS[:, bank:bank + 2, 0:HALF]
            return PS[:, bank, 0:n]

        def as_halves(ap, n=T):
            return ap.rearrange("p (h t) -> p h t", h=2) if n == T else ap

        def segs(n=T):
            return ((0, L, 0), (L, T, 1)) if n == T else ((0, L, 0),)

        consts_in = sem("consts_in")
        params_in = sem("params_in")
        x_in = sem("x_in")
        params_T = sem("params_T")
        params_ready = sem("params_ready")
        x_T = sem("x_T")
        x_evicted = sem("x_evicted")
        c_silu = sem("c_silu")
        mod_full = [sem(f"mod_full{s}") for s in range(3)]
        mod_mm = sem("mod_mm")
        mod_row = sem("mod_row")
        mod_cols = sem("mod_cols")
        mod_added = sem("mod_added")
        gains_ready = sem("gains_ready")
        w_full = [sem(f"w_full{s}") for s in range(SLOTS)]
        slots_used = sem("slots_used")
        sq_ready = sem("sq_ready")
        sq_used = sem("sq_used")
        root_ready = sem("root_ready")
        rstd_ready = sem("rstd_ready")
        scaled = sem("scaled")
        normed = sem("normed")
        x_updated = sem("x_updated")
        dve_step = sem("dve_step")
        act_step = sem("act_step")
        out_T = sem("out_T")
        out_sb = sem("out_sb")
        stored = sem("stored")

        SQ, ROOT, SCL, GATE, _ = carve(TMP, [2 * T, T, 2 * T, 2 * T, 0])
        SQ = SQ.rearrange("p (s t) -> p s t", s=2)
        SCL = SCL.rearrange("p (s t) -> p s t", s=2)
        GATE = GATE.rearrange("p (s t) -> p s t", s=2)

        class Dense:
            def __init__(self, name, kind, groups, base, w, rhs, dest, n=T):
                self.kind, self.groups, self.base, self.w, self.rhs, self.dest, self.n = \
                    kind, groups, base, w, rhs, dest, n
                self.units = 4 if kind == "plain" else 2
                self.unit_free = sem(name + "_banks_free")
                self.done = groups * self.units + self.units

        def tile_of_weights(w, m, k0, k1):
            v = w.rearrange("(k p) (m c) -> m p k c", p=128, c=128)
            return v[bass.ds(m, 1), :, k0:k1, :].rearrange("a p k c -> (a p) k c")

        def dense_load(sp, d, first=False):
            def group(i, wait):
                for s in range(SLOTS):
                    if wait:
                        sp.wait_ge(slots_used, 4 * (d.base - 1) + 4 * i + s + 1)
                    if d.kind == "plain":
                        sp.dma_start(WR[:, s, 0:CT, :], tile_of_weights(d.w, 4 * i + s, 0, CT))\
                          .then_inc(w_full[s], 16)
                    elif d.kind == "gate":
                        sp.dma_start(WR[:, s, 0:CT, :], tile_of_weights(d.w[s % 2], 2 * i + s // 2, 0, CT))\
                          .then_inc(w_full[s], 16)
                    else:
                        k0 = SLOT_K * (s % 2)
                        sp.dma_start(WR[:, s, :, :], tile_of_weights(d.w, 2 * i + s // 2, k0, k0 + SLOT_K))\
                          .then_inc(w_full[s], 16)
            if first:
                group(0, False)
            with sp.Fori(1 if first else 0, d.groups) as i:
                group(i, True)

        def dense_pe(pe, d):
            with pe.Fori(0, d.groups) as i:
                for s in range(SLOTS):
                    u = s if d.kind == "plain" else s // 2
                    bank = 2 * s if d.kind != "long" else 4 * u
                    begins = d.kind != "long" or s % 2 == 0
                    ends = d.kind != "long" or s % 2 == 1
                    if d.kind == "plain" or s % 2 == 0:
                        pe.wait_ge(d.unit_free, d.units * i + u + 1)
                    pe.wait_ge(w_full[s], 16 * (i + d.base + 1))
                    k0, kn = (SLOT_K * (s % 2), SLOT_K) if d.kind == "long" else (0, CT)
                    for k in range(kn):
                        for h0, h1, b in (((0, HALF, 0), (HALF, T, 1)) if d.n == T else ((0, L, 0),)):
                            last = nc.tensor.matmul(
                                PS[:, bank + b, 0:h1 - h0], WR[:, s, k, :], d.rhs(k0 + k)[:, h0:h1],
                                start=begins and k == 0, stop=ends and k == kn - 1)
                    last.then_inc(slots_used, 1)

        def dense_evict_act(act, d):
            if d.kind != "gate":
                act.sem_inc(d.unit_free, d.units)
            with act.Fori(0, d.groups) as i:
                for u in range(d.units):
                    last_slot = u if d.kind == "plain" else (2 * u if d.kind == "gate" else 2 * u + 1)
                    bank = 2 * u if d.kind == "plain" else 4 * u
                    act.wait_ge(slots_used, 4 * d.base + 4 * i + last_slot + 1)
                    if d.kind == "gate":
                        nc.scalar.activation(as_halves(GATE[:, u, 0:d.n], d.n), halves(bank, d.n), ACT.Silu)\
                          .then_inc(silu_ready, 1)
                    else:
                        act.wait_ge(consts_in, CONST_DMAS)
                        dst = d.dest[:, bass.ds(d.units * i + u, 1), 0:d.n].rearrange("p a t -> p (a t)")
                        nc.scalar.activation(as_halves(dst, d.n), halves(bank, d.n), ACT.Copy)\
                          .then_inc(d.unit_free, 1)

        def gate_evict_dve(v, d, silu_base):
            v.sem_inc(d.unit_free, d.units)
            with v.Fori(0, d.groups) as i:
                for u in range(2):
                    v.wait_ge(slots_used, 4 * d.base + 4 * i + 2 * u + 2)
                    v.wait_ge(silu_ready, silu_base + 2 * i + u + 1)
                    dst = d.dest[:, bass.ds(2 * i + u, 1), 0:d.n].rearrange("p a t -> p (a t)")
                    nc.vector.tensor_tensor(as_halves(dst, d.n), as_halves(GATE[:, u, 0:d.n], d.n),
                                            halves(4 * u + 2, d.n), ALU.mult).then_inc(d.unit_free, 1)

        silu_ready = sem("silu_ready")

        def norm_squares_act(act, q, src, n, ready):
            for t in range(CT):
                ready(act, t)
                if t >= 2 or q > 0:
                    act.wait_ge(sq_used, q * CT + t - 1)
                nc.scalar.activation(SQ[:, t % 2, 0:n], src(t), ACT.Square).then_inc(sq_ready, 1)
            act.wait_ge(sq_used, q * CT + CT)
            nc.scalar.activation(as_halves(ROOT[:, 0:n], n), halves(0, n), ACT.Sqrt, bias=small[:, 0:1])\
              .then_inc(root_ready, 1)

        def norm_pe(pe, q, n, before):
            before(pe)
            for t in range(CT):
                pe.wait_ge(sq_ready, q * CT + t + 1)
                for h0, h1, b in (((0, HALF, 0), (HALF, T, 1)) if n == T else ((0, L, 0),)):
                    last = nc.tensor.matmul(PS[:, b, 0:h1 - h0], ones[:, :], SQ[:, t % 2, h0:h1],
                                            start=t == 0, stop=t == CT - 1)
                last.then_inc(sq_used, 1)

        def norm_scale_dve(v, q, src, n, scaled_base=None, residual=None):
            v.wait_ge(root_ready, q + 1)
            nc.vector.reciprocal(halves(2, n), as_halves(ROOT[:, 0:n], n)).then_inc(rstd_ready, 1)
            v.wait_ge(rstd_ready, q + 1)
            for t in range(CT):
                if residual is None and t >= 2:
                    v.wait_ge(normed, NORMED_BASE[q] + t - 1)
                ins = nc.vector.tensor_tensor(as_halves(SCL[:, t % 2, 0:n], n), as_halves(src(t), n),
                                              halves(2, n), ALU.mult)
                ins.then_inc(scaled, 1)
                if residual is not None:
                    v.wait_ge(scaled, q * CT + t + 1)
                    l, k = residual
                    for s0, s1, w in segs(n):
                        last = nc.vector.scalar_tensor_tensor(
                            X[:, t, s0:s1], SCL[:, t % 2, s0:s1], DER[:, l, k, w, t:t + 1], X[:, t, s0:s1],
                            ALU.mult, ALU.add)
                    last.then_inc(x_updated, 1)

        def norm_shift_act(act, q, n, l, k, dest):
            for t in range(CT):
                act.wait_ge(scaled, q * CT + t + 1)
                for s0, s1, w in segs(n):
                    j = (0 if k == 0 else 24) + t
                    last = nc.scalar.activation(dest(t, s0, s1), SCL[:, t % 2, s0:s1], ACT.Identity,
                                                bias=modT[:, l, j, w:w + 1], scale=DER[:, l, k, w, t:t + 1])
                last.then_inc(normed, 1)

        NORMED_BASE = {0: 0, 2: 8, 4: 16, 6: 24}

        class Chain:
            def __init__(self, eng, s, per=0):
                self.eng, self.s, self.per, self.k, self.turn = eng, s, per, 0, 0

            def start(self, i):
                assert i is None or self.k in (0, self.per), (self.k, self.per)
                self.turn, self.k = i * self.per, 0

            def link(self, ins):
                self.k += 1
                ins.then_inc(self.s, 1)
                self.eng.wait_ge(self.s, self.turn + self.k)

            def end(self):
                assert self.k == self.per, (self.k, self.per)

        passed = sem("passed")

        QP, KP, VP, VT, SC, ST = carve(WRf, [T, T, T, T, 2 * T, 16])
        SC = SC.rearrange("p (s t) -> p s t", s=2)
        VT = VT.rearrange("p (k c) -> p k c", k=6)
        ND = 2 * ROWS - 1
        BIAS, BP = carve(TMP, [NH * ND * GRID, 2 * ND * GRID])
        BIAS = BIAS.rearrange("p (x j) -> p x j", j=GRID)
        PT, PTC, RPL, RP, PICK, WINDOW = carve(Yf, [6 * L, 2 * C, 2 * WIN - 1, NH * ND, 3 * GRID - 1, GRID])
        PT = PT.rearrange("p (k t) -> p k t", k=6)
        PTC = PTC.rearrange("p (k t) -> p k t", k=2)
        ITEMS = [(hh, t) for hh in range(2) for t in range(6)]

        bias_in = sem("bias_in")
        rpb_T = sem("rpb_T")
        rpb_ready = sem("rpb_ready")
        bias_mm = sem("bias_mm")
        bias_ready = sem("bias_ready")
        values_in = sem("values_in")
        pair_in = sem("pair_in")
        scores_done = sem("scores_done")
        max_ready = sem("max_ready")
        exp_done = sem("exp_done")
        probs_ready = sem("probs_ready")
        tr_done = sem("tr_done")
        tr_evicted = sem("tr_evicted")
        pv_done = sem("pv_done")
        attn_out = sem("attn_out")
        attn_step = sem("attn_step")

        def bias_pe(pe):
            pe.wait_ge(bias_in, 48)
            pe.wait_ge(inproj.unit_free, inproj.done)
            nc.tensor.transpose(PS[0:2 * WIN - 1, 0, 0:NH * ND], RPL[0:NH * ND, :], ident[0:NH * ND, 0:NH * ND])\
              .then_inc(rpb_T, 1)
            pe.wait_ge(rpb_ready, 3)
            for g in range(GRID // 4):
                if g >= 4:
                    pe.wait_ge(bias_ready, g - 3)
                for q in range(4):
                    j = 4 * g + q
                    last = nc.tensor.matmul(PS[:, 4 + g % 4, 120 * q:120 * q + 120],
                                            PICK[0:64, GRID - 1 - j:3 * GRID - 1 - j], RP[0:64, :],
                                            start=True, stop=True)
                last.then_inc(bias_mm, 1)

        def bias_dve(v):
            v.wait_ge(x_T, 8)
            v.wait_ge(x_evicted, 8)
            nc.vector.memset(RP[0:64, :], 0.0).then_inc(rpb_ready, 1)
            v.wait_ge(rpb_ready, 1)
            v.wait_ge(rpb_T, 1)
            rp = RP.rearrange("p (h d) -> p h d", h=NH)
            src = PS[0:2 * WIN - 1, 0, 0:NH * ND].rearrange("p (h d) -> p h d", h=NH)
            nc.vector.tensor_copy(rp[0:2 * WIN - 1, :, :], src).then_inc(rpb_ready, 1)
            nc.vector.tensor_copy(rp[32:32 + 2 * WIN - 1, :, 1:ND], src[:, :, 0:ND - 1]).then_inc(rpb_ready, 1)
            for g in range(GRID // 4):
                v.wait_ge(bias_mm, g + 1)
                w = WINDOW[:, 4 * g:4 * g + 4].unsqueeze(1).broadcast_to([128, 120, 4])
                nc.vector.tensor_tensor(BIAS[:, :, 4 * g:4 * g + 4],
                                        PS[:, 4 + g % 4, 0:480].rearrange("p (q x) -> p x q", q=4), w, ALU.add)\
                  .then_inc(bias_ready, 1)

        def attn_pool(pool):
            pool.wait_ge(inproj.unit_free, inproj.done)
            with pool.Fori(0, NH // 2) as i:
                pool.wait_ge(tr_done, 13 * i + 2)
                pool.sem_inc(passed, 1)
                nc.gpsimd.tensor_copy(VP, P[:, bass.ds(8 + i, 1), :].rearrange("p a t -> p (a t)"))\
                  .then_inc(values_in, 1)

        def attn_pe(pe):
            pe.sem_inc(tr_done, 2)
            pe.sem_inc(pv_done, 4)

            def scores(i, n):
                hh, t = ITEMS[n]
                r = slice(64 * hh, 64 * hh + 64)
                pe.wait_ge(exp_done, 12 * i + n + 1)
                if t < 4:
                    nc.tensor.matmul(PS[:, n % 2, 0:L], QP[r, 128 * t:128 * t + 128], KP[r, 0:L],
                                     start=True, stop=True)
                nc.tensor.matmul(PS[:, 2 + n % 2, 0:C], QP[r, 128 * t:128 * t + 128], KP[r, L:T],
                                 start=True, stop=True).then_inc(scores_done, 1)

            def transposes(i, n):
                hh, t = ITEMS[n]
                pe.wait_ge(tr_evicted, 13 * i + n + 2)
                pe.wait_ge(probs_ready, 12 * i + n + 1)
                for k in range(6 if t < 4 else 2):
                    at = 128 * k if t < 4 else L + 128 * k
                    last = nc.tensor.transpose(PS[:, 4 + k // 3, 128 * (k % 3):128 * (k % 3) + 128],
                                               SC[:, n % 2, at:at + 128], ident[:, :])
                last.then_inc(tr_done, 1)

            def latent_out(i, hh):
                if hh == 0:
                    pe.wait_ge(attn_out, 2 * i + 2)
                pe.wait_ge(tr_evicted, 13 * i + 6 * hh + 4 + 2)
                for k in range(6):
                    last = nc.tensor.matmul(PS[64 * hh:64 * hh + 64, 6, 0:L], VT[:, k, 64 * hh:64 * hh + 64],
                                            PT[:, k, :], start=k == 0, stop=k == 5)
                last.then_inc(pv_done, 1)

            def context_out(i, hh):
                pe.wait_ge(tr_evicted, 13 * i + 6 * hh + 6 + 2)
                for k in range(2):
                    last = nc.tensor.matmul(PS[64 * hh:64 * hh + 64, 7, 0:C], VT[:, 4 + k, 64 * hh:64 * hh + 64],
                                            PTC[:, k, :], start=k == 0, stop=k == 1)
                last.then_inc(pv_done, 1)

            pe.wait_ge(bias_ready, GRID // 4)
            with pe.Fori(0, NH // 2) as i:
                pe.wait_ge(pair_in, 2 * i + 2)
                scores(i, 0)
                pe.wait_ge(values_in, i + 1)
                pe.wait_ge(tr_evicted, 13 * i + 1)
                for k in range(6):
                    last = nc.tensor.transpose(PS[:, 4 + k // 3, 128 * (k % 3):128 * (k % 3) + 128],
                                               VP[:, 128 * k:128 * k + 128], ident[:, :])
                last.then_inc(tr_done, 1)
                for n in range(12):
                    if n < 11:
                        scores(i, n + 1)
                    transposes(i, n)
                    if n % 6 == 4:
                        latent_out(i, n // 6)
                    if n == 6:
                        context_out(i, 0)
                context_out(i, 1)

        def attn_act(act):
            act.sem_inc(exp_done, 2)
            act.sem_inc(tr_evicted, 1)

            def evict(i, n):
                hh, t = ITEMS[n]
                if t in (0, 4):
                    act.wait_ge(pv_done, 4 * i + (3 if t == 0 else 4) + 2 * hh)
                act.wait_ge(tr_done, 13 * i + n + 4)
                if t < 4:
                    nc.scalar.activation(PT[:, :, 128 * t:128 * t + 128].rearrange("p (h k) c -> p h k c", h=2),
                                         halves(4).rearrange("p h (k c) -> p h k c", k=3), ACT.Copy)\
                      .then_inc(tr_evicted, 1)
                else:
                    nc.scalar.activation(PTC[:, :, 128 * (t - 4):128 * (t - 4) + 128],
                                         PS[:, 4, 0:256].rearrange("p (k c) -> p k c", k=2), ACT.Copy)\
                      .then_inc(tr_evicted, 1)

            act.wait_ge(inproj.unit_free, inproj.done)
            with act.Fori(0, NH // 2) as i:
                for dst, at, by in ((QP, 0, CH ** -0.5), (KP, 4, 1.0)):
                    nc.scalar.activation(dst, P[:, bass.ds(at + i, 1), :].rearrange("p a t -> p (a t)"), ACT.Copy,
                                         scale=by).then_inc(pair_in, 1)
                for n, (hh, t) in enumerate(ITEMS):
                    st = ST[:, 8 * (n % 2):8 * (n % 2) + 8]
                    act.wait_ge(max_ready, 12 * i + n + 1)
                    if t < 4:
                        nc.scalar.activation(SC[:, n % 2, 0:L], SC[:, n % 2, 0:L], ACT.Exp, bias=st[:, 2:3],
                                             accum_out=st[:, 3:4])
                    nc.scalar.activation(SC[:, n % 2, L:T], PS[:, 2 + n % 2, 0:C], ACT.Exp, bias=st[:, 2:3],
                                         accum_out=st[:, 4:5]).then_inc(exp_done, 1)
                    if n == 0:
                        act.wait_ge(tr_done, 13 * i + 3)
                        act.wait_ge(pv_done, 4 * i + 4)
                        nc.scalar.activation(VT[:, :, :].rearrange("p (h k) c -> p h k c", h=2),
                                             halves(4).rearrange("p h (k c) -> p h k c", k=3), ACT.Copy)\
                          .then_inc(tr_evicted, 1)
                    else:
                        evict(i, n - 1)
                evict(i, 11)

        ATTN_LINKS = 1 + 8 * 4 + 4 * 3

        def attn_dve(v):
            v.sem_inc(attn_out, 2)
            v.wait_ge(bias_ready, GRID // 4)
            chain = Chain(v, attn_step, ATTN_LINKS)

            def maximum(i, n):
                hh, t = ITEMS[n]
                st = ST[:, 8 * (n % 2):8 * (n % 2) + 8]
                v.wait_ge(scores_done, 12 * i + n + 1)
                v.wait_ge(tr_done, 13 * i + n + (2 if n >= 2 else 1))
                v.sem_inc(passed, 1)
                if t < 4:
                    bp = BP[:, (hh * ND + 7 - 2 * t) * GRID:(hh * ND + 15 - 2 * t) * GRID]
                    ins = nc.vector.tensor_tensor_reduce(
                        out=SC[:, n % 2, 0:L], in0=PS[:, n % 2, 0:L], in1=bp, scale=1.0, scalar=-3e38,
                        op0=ALU.add, op1=ALU.max, accum_out=st[:, 0:1])
                    chain.link(ins)
                    chain.link(nc.vector.reduce_max(st[:, 1:2], PS[:, 2 + n % 2, 0:C], AX_X))
                    nc.vector.scalar_tensor_tensor(st[:, 2:3], st[:, 0:1], st[:, 1:2], small[:, 1:2],
                                                   ALU.max, ALU.mult).then_inc(max_ready, 1)
                else:
                    chain.link(nc.vector.reduce_max(st[:, 1:2], PS[:, 2 + n % 2, 0:C], AX_X))
                    nc.vector.tensor_scalar(st[:, 2:3], st[:, 1:2], -1.0, None, ALU.mult).then_inc(max_ready, 1)

            def normalise(i, n):
                hh, t = ITEMS[n]
                st = ST[:, 8 * (n % 2):8 * (n % 2) + 8]
                v.wait_ge(exp_done, 12 * i + n + 3)
                if t < 4:
                    chain.link(nc.vector.tensor_tensor(st[:, 5:6], st[:, 3:4], st[:, 4:5], ALU.add))
                else:
                    chain.link(nc.vector.tensor_copy(st[:, 5:6], st[:, 4:5]))
                chain.link(nc.vector.reciprocal(st[:, 6:7], st[:, 5:6]))
                at = 0 if t < 4 else L
                nc.vector.tensor_scalar(SC[:, n % 2, at:T], SC[:, n % 2, at:T], st[:, 6:7], None, ALU.mult)\
                  .then_inc(probs_ready, 1)

            with v.Fori(0, NH // 2) as i:
                chain.start(i)
                chain.link(nc.vector.tensor_scalar(BP.rearrange("p (x j) -> p x j", j=GRID),
                                                   BIAS[:, bass.ds(2 * ND * i, 2 * ND), :], 1.0, None, ALU.mult))
                maximum(i, 0)
                for n in range(12):
                    normalise(i, n)
                    if n < 11:
                        maximum(i, n + 1)
                v.wait_ge(pv_done, 4 * i + 8)
                for b, s0, s1 in ((6, 0, L), (7, L, T)):
                    nc.vector.tensor_scalar(H[:, bass.ds(i, 1), s0:s1].rearrange("p a t -> p (a t)"),
                                            PS[:, b, 0:s1 - s0], 1.0, None, ALU.mult).then_inc(attn_out, 1)
                chain.end()

        RUNS = [(L, 0, 0, 0), (L, 0, 1, 1), (C, L, 0, 2), (C, L, 1, 3)]
        CUM = [0, 4, 8, 10, 12]
        HYA = Pf[:, 12 * T:24 * T]
        HPM, ZT, T4, DEC = carve(HYA, [2 * 4 * HW, 4 * HW, 4 * HW, 2 * HW])
        HPM = HPM.rearrange("p (a k w) -> p a k w", a=2, k=4)
        YRI = HPM
        ZT = ZT.rearrange("p (k w) -> p k w", k=4)
        T4 = T4.rearrange("p (a w) -> p a w", a=4)
        DEC = DEC.rearrange("p (a w) -> p a w", a=2)
        DF, HIDT, DELTA, TIMES, PW1, PW2, PM, RN = carve(TMP, [8192, T, HW, 12, HID, HID, 4, 8])
        PW3, AB = carve(Yf, [4 * HW, 8 * HW])
        AB = AB.rearrange("p (a k w) -> p a k w", a=2, k=4)
        FEATS, ARG, KR = ZT[:, 0:2, :].rearrange("p k w -> p (k w)")[:, 0:T], \
            HPM[:, 0, 0:2, :].rearrange("p k w -> p (k w)")[:, 0:T], \
            HPM[:, 1, 0:2, :].rearrange("p k w -> p (k w)")[:, 0:T]
        HIDP = AB[:, 0, 0:2, :].rearrange("p k w -> p (k w)")[:, 0:T]

        def dft(n):
            return DF[:, 0:4 * (n // 128) * n].rearrange("p (a k f) -> p a k f", a=4, k=n // 128)

        hy_in = sem("hy_in")
        dft_in = sem("dft_in")
        feats_in = sem("feats_in")
        conv3_done = sem("conv3_done")
        conv3_step = sem("conv3_step")
        mlp_mm = sem("mlp_mm")
        mlp_arg = sem("mlp_arg")
        mlp_hid = sem("mlp_hid")
        filt_mm = sem("filt_mm")
        dec_ready = sem("dec_ready")
        hpm_ready = sem("hpm_ready")
        abs_ready = sem("abs_ready")
        sum_used = sem("sum_used")
        row_ready = sem("row_ready")
        rn_T = sem("rn_T")
        rn_ready = sem("rn_ready")
        ab_mm = sem("ab_mm")
        ab_ready = sem("ab_ready")
        zt_mm = sem("zt_mm")
        zt_ready = sem("zt_ready")
        z_mm = sem("z_mm")
        zmul_done = sem("zmul_done")
        y_ready = sem("y_ready")
        conv_mm = sem("conv_mm")
        z_done = sem("z_done")

        def hyena_sp(sp):
            sp.wait_ge(attn_out, 2 + NH)
            for dst, src in ((HIDT_IN[0], a["deltas"]), (TIMES, a["times"]), (PW1[0:EMB, :], a["hy_pos_w1"][0]),
                             (PW2[0:HID, :], a["hy_pos_w2"][0]), (PW3[0:HID, :], a["hy_pos_w3"][0]),
                             (PM[0:HID, 0:1], a["hy_pos_b1"].rearrange("a n -> n a")),
                             (PM[0:HID, 1:2], a["hy_pos_b2"].rearrange("a n -> n a")),
                             (PM[0:HID, 2:3], a["hy_sin_freq"].rearrange("a n -> n a"))):
                sp.dma_start(dst, src).then_inc(hy_in, 16)
            sp.dma_start(dft(L), a["dft512"]).then_inc(dft_in, 16)
            sp.wait_ge(conv3_done, 12)
            sp.dma_start(FEATS[0:EMB, :], a["feats"]).then_inc(feats_in, 16)
            sp.wait_ge(conv_mm, 8)
            sp.dma_start(dft(C), a["dft256"]).then_inc(dft_in, 16)

        HIDT_IN = [DELTA]

        def conv3_dve(v):
            chain = Chain(v, conv3_step, 2)
            v.wait_ge(params_ready, 4)
            with v.Fori(0, 12) as i:
                chain.start(i)
                src = P[:, bass.ds(12 + i, 1), :].rearrange("p a t -> p (a t)")
                dst = P[:, bass.ds(i, 1), :].rearrange("p a t -> p (a t)")

                def w(tap):
                    return PC[:, bass.ds(SW_COL + 12 * tap + i, 1)]
                chain.link(nc.vector.tensor_scalar(dst, src, w(1), PC[:, bass.ds(SB_COL + i, 1)], ALU.mult, ALU.add))
                for s0, s1, _ in segs():
                    ins = nc.vector.scalar_tensor_tensor(dst[:, s0 + 1:s1], src[:, s0:s1 - 1], w(0),
                                                         dst[:, s0 + 1:s1], ALU.mult, ALU.add)
                chain.link(ins)
                for s0, s1, _ in segs():
                    ins = nc.vector.scalar_tensor_tensor(dst[:, s0:s1 - 1], src[:, s0 + 1:s1], w(2),
                                                         dst[:, s0:s1 - 1], ALU.mult, ALU.add)
                ins.then_inc(conv3_done, 1)
                chain.end()

        def mlp_pe(pe):
            for k, (w, x) in enumerate(((PW1[0:EMB, :], FEATS[0:EMB, :]), (PW2[0:HID, :], HIDP[0:HID, :]))):
                pe.wait_ge(hy_in, 16 * 8)
                pe.wait_ge(feats_in, 16)
                if k:
                    pe.wait_ge(mlp_hid, 1)
                for h in range(2):
                    last = nc.tensor.matmul(PS[0:HID, h, 0:HALF], w, x[:, HALF * h:HALF * h + HALF],
                                            start=True, stop=True)
                last.then_inc(mlp_mm, 1)

        def mlp_dve(v, chain):
            for k in range(2):
                v.wait_ge(mlp_mm, k + 1)
                h = slice(0, HID)
                chain.link(nc.vector.tensor_scalar(as_halves(ARG[h, :]), PS[h, 0:2, 0:HALF], PM[h, k:k + 1],
                                                   PM[h, 2:3], ALU.add, ALU.mult))
                magic = 12582912.0
                chain.link(nc.vector.tensor_scalar(KR[h, :], ARG[h, :], 1.0 / (2 * PI), magic, ALU.mult, ALU.add))
                chain.link(nc.vector.tensor_scalar(KR[h, :], KR[h, :], magic, None, ALU.subtract))
                for c in (6.28125, 1.93500518798828125e-3, 3.0199159819e-7):
                    chain.link(nc.vector.scalar_tensor_tensor(ARG[h, :], KR[h, :], -c, ARG[h, :],
                                                              ALU.mult, ALU.add))
                nc.vector.tensor_scalar(ARG[h, :], ARG[h, :], 3.1415925, -3.1415925, ALU.min, ALU.max)\
                  .then_inc(mlp_arg, 1)

        def mlp_act(act):
            for k, dst in enumerate((HIDP, HIDT)):
                act.wait_ge(mlp_arg, k + 1)
                nc.scalar.activation(dst[0:HID, :], ARG[0:HID, :], ACT.Sin).then_inc(mlp_hid, 1)

        def hyena_pe(pe):
            for n, first, o, r in RUNS:
                nt, cum = n // 128, CUM[r]
                m = dft(n)
                pe.wait_ge(mlp_hid, 2)
                for k in range(nt):
                    if r:
                        pe.wait_ge(z_done, 4 * r)
                    if k >= 2:
                        pe.wait_ge(hpm_ready, cum + k - 1)
                    for d in range(2):
                        last = nc.tensor.matmul(
                            PS[:, 2 * (k % 2) + d, 0:HW], HIDT[0:HID, first + 128 * k:first + 128 * k + 128],
                            PW3[0:HID, (2 * d + o) * HW:(2 * d + o + 1) * HW], start=True, stop=True)
                    last.then_inc(filt_mm, 1)
                for k in range(nt):
                    pe.wait_ge(abs_ready, cum + k + 1)
                    for d in range(2):
                        last = nc.tensor.matmul(PS[0:1, 4, 0:HW], ones[:, 0:1], T4[:, 2 * (k % 2) + d, :],
                                                start=k + d == 0, stop=k == nt - 1 and d == 1)
                    last.then_inc(sum_used, 1)
                pe.wait_ge(dft_in, 16 if n == L else 32)
                pe.wait_ge(hpm_ready, cum + nt)
                for f in range(nt):
                    if f >= 2:
                        pe.wait_ge(ab_ready, cum + f - 1)
                    for p in range(2):
                        for k in range(nt):
                            last = nc.tensor.matmul(PS[:, 2 * (f % 2) + p, 0:HW], m[:, p, k, 128 * f:128 * f + 128],
                                                    HPM[:, p, k, :], start=k == 0, stop=k == nt - 1)
                    last.then_inc(ab_mm, 1)
                pe.wait_ge(row_ready, r + 1)
                for c in range(4):
                    last = nc.tensor.transpose(PS[:, 5, c:c + 1], DEC[0:1, 0, 128 * c:128 * c + 128], ident[0:1, 0:1])
                last.then_inc(rn_T, 1)
                for k in range(nt):
                    if k >= 2:
                        pe.wait_ge(zt_ready, cum + k - 1)
                    for c in range(4):
                        last = nc.tensor.transpose(PS[:, 6 + k % 2, 128 * c:128 * c + 128],
                                                   P[:, c, first + 128 * k:first + 128 * k + 128], ident[:, :])
                    last.then_inc(zt_mm, 1)
                pe.wait_ge(ab_ready, cum + nt)
                pe.wait_ge(zt_ready, cum + nt)
                for f in range(nt):
                    if f >= 2:
                        pe.wait_ge(zmul_done, cum + f - 1)
                    for p in range(2):
                        for k in range(nt):
                            last = nc.tensor.matmul(PS[:, 2 * (f % 2) + p, 0:HW], m[:, p, k, 128 * f:128 * f + 128],
                                                    ZT[:, k, :], start=k == 0, stop=k == nt - 1)
                    last.then_inc(z_mm, 1)
                pe.wait_ge(rn_ready, r + 1)
                pe.wait_ge(y_ready, cum + nt)
                for c in range(4):
                    for p in range(2):
                        for f in range(nt):
                            last = nc.tensor.matmul(PS[:, 4 + c, 0:n], YRI[:, p, f, 128 * c:128 * c + 128],
                                                    m[:, 2 + p, f, :], start=p + f == 0,
                                                    stop=p == 1 and f == nt - 1)
                    last.then_inc(conv_mm, 1)

        def hyena_act(act):
            act.wait_ge(hy_in, 16 * 8)
            for n, first, o, r in RUNS:
                nt, cum = n // 128, CUM[r]
                tcol = 0 if n == L else 8

                def decays(k):
                    if cum + k:
                        act.wait_ge(hpm_ready, cum + k)
                    if r and k == 0:
                        act.wait_ge(rn_T, r)
                    for d in range(2):
                        last = nc.scalar.activation(DEC[:, d, :], DELTA, ACT.Exp,
                                                    scale=TIMES[:, tcol + nt * d + k:tcol + nt * d + k + 1])
                    last.then_inc(dec_ready, 1)

                for k in range(nt):
                    decays(k)
                    act.wait_ge(hpm_ready, cum + k + 1)
                    for d in range(2):
                        x = T4[:, 2 * (k % 2) + d, :]
                        last = nc.scalar.activation(x, x, ACT.Abs)
                    last.then_inc(abs_ready, 1)
                for f in range(nt):
                    act.wait_ge(ab_mm, cum + f + 1)
                    nc.scalar.activation(AB[:, :, f, :], PS[:, 2 * (f % 2):2 * (f % 2) + 2, 0:HW], ACT.Copy)\
                      .then_inc(ab_ready, 1)
                for k in range(nt):
                    act.wait_ge(zt_mm, cum + k + 1)
                    nc.scalar.activation(ZT[:, k, :], PS[:, 6 + k % 2, 0:HW], ACT.Copy).then_inc(zt_ready, 1)

        def hyena_dve(v, chain):
            for n, first, o, r in RUNS:
                nt, cum = n // 128, CUM[r]
                for k in range(nt):
                    v.wait_ge(filt_mm, cum + k + 1)
                    v.wait_ge(dec_ready, cum + k + 1)
                    if k >= 2:
                        v.wait_ge(sum_used, cum + k - 1)
                    b = 2 * (k % 2)
                    chain.link(nc.vector.tensor_tensor(T4[:, b:b + 2, :], DEC[:, :, :], PS[:, b:b + 2, 0:HW], ALU.mult))
                    nc.vector.tensor_tensor(HPM[:, 0, k, :], T4[:, b, :], T4[:, b + 1, :], ALU.add)
                    nc.vector.tensor_tensor(HPM[:, 1, k, :], T4[:, b, :], T4[:, b + 1, :], ALU.subtract)\
                      .then_inc(hpm_ready, 1)
                v.wait_ge(sum_used, cum + nt)
                nc.vector.tensor_copy(DEC[0:1, 0, :], PS[0:1, 4, 0:HW]).then_inc(row_ready, 1)
                v.wait_ge(rn_T, r + 1)
                chain.link(nc.vector.reciprocal(RN[:, 4:8], PS[:, 5, 0:4]))
                nc.vector.tensor_scalar(RN[:, 0:4], RN[:, 4:8], 1.0 / D, None, ALU.mult).then_inc(rn_ready, 1)
                v.wait_ge(rn_ready, r + 1)
                v.wait_ge(ab_ready, cum + nt)
                for f in range(nt):
                    v.wait_ge(z_mm, cum + f + 1)
                    b = 2 * (f % 2)
                    if f:
                        v.wait_ge(y_ready, cum + f)
                    nc.vector.tensor_tensor(T4[:, 0:2, :], AB[:, :, f, :], PS[:, b:b + 2, 0:HW], ALU.mult)
                    for p in range(2):
                        ins = nc.vector.tensor_tensor(T4[:, 2 + p, :], AB[:, 1 - p, f, :], PS[:, b + p, 0:HW], ALU.mult)
                    ins.then_inc(zmul_done, 1)
                    v.wait_ge(zmul_done, cum + f + 1)
                    nc.vector.tensor_tensor(YRI[:, 0, f, :], T4[:, 0, :], T4[:, 1, :], ALU.subtract)
                    nc.vector.tensor_tensor(YRI[:, 1, f, :], T4[:, 2, :], T4[:, 3, :], ALU.add).then_inc(y_ready, 1)
                for c in range(4):
                    v.wait_ge(conv_mm, 4 * r + c + 1)
                    tmp = ZT[:, c, 0:n]
                    z = P[:, c, first:first + n]
                    gate = P[:, 4 + 4 * o + c, first:first + n]
                    chain.link(nc.vector.tensor_scalar(tmp, PS[:, 4 + c, 0:n], RN[:, c:c + 1], None, ALU.mult))
                    chain.link(nc.vector.scalar_tensor_tensor(tmp, z, col(SKIP_COL + 4 * o + c), tmp,
                                                              ALU.mult, ALU.add))
                    dst = z if o == 0 else H[:, 4 + c, first:first + n]
                    nc.vector.tensor_tensor(dst, tmp, gate, ALU.mult).then_inc(z_done, 1)

        PR = carve(Yf, [T * CT])[0]
        XT = Yf.rearrange("p (k d) -> p k d", k=6)
        ROWS4 = Hraw[:, 0:512].rearrange("p (a c) -> p a c", a=4)
        CS = Hraw[:, 512:528]
        MROW = Hraw[:, 1024:1024 + 3 * 512].rearrange("p (s n) -> p s n", s=3)
        MW = Pf[:, 0:3 * 4096].rearrange("p (s k n) -> p s k n", s=3, k=CT)
        CONST_DMAS = 16 * 2

        def rows(x):
            names = " ".join("abcd"[:len(x.shape) - 1])
            return x.rearrange(f"{names} (k c) -> ({names} k) c", c=128)

        def inputs_sp(sp):
            for dst, name in ((ident, "ident"), (ones, "ones")):
                sp.dma_start(dst[:, :], a[name]).then_inc(consts_in, 16)
            lists = (("c", "c_ctx", "norm_g"), ("mod_b",), ("hy_short_w", "hy_short_b", "hy_skip", "rw_mu"),
                     ("rw_w0", "rw_a0", "rw_k_k", "rw_k_a", "rw_r_k", "rw_ln_w", "rw_ln_b"))
            for q, names in enumerate(lists):
                at = 0
                for name in names:
                    x = a[name]
                    if name == "c_ctx":
                        src = x.rearrange("(k c) -> k c", c=128)
                    elif name == "rw_r_k":
                        src = x.rearrange("z e (k h) n -> (z e k) (h n)", h=2)
                    else:
                        src = rows(x)
                    sp.dma_start(ROWS4[at:at + src.shape[0], q, :], src).then_inc(params_in, 16)
                    at += src.shape[0]
                assert at == NROWS[q], (at, q)

            v = a["mod_w"].rearrange("l (k p) (b n) -> l b p k n", p=128, n=512)

            def block(l, b, s):
                sp.dma_start(MW[:, s, :, :], v[l][bass.ds(b, 1)].rearrange("a p k n -> (a p) k n"))\
                  .then_inc(mod_full[s], 16)

            for s in range(3):
                block(0, s, s)
            sp.dma_start(XT[:, 0:4, :], a["x"][0].rearrange("(k p) d -> p k d", p=128)).then_inc(x_in, 16)
            sp.dma_start(XT[:, 4:6, :], a["ctx"][0].rearrange("(k p) d -> p k d", p=128)).then_inc(x_in, 16)
            for l in range(2):
                with sp.Fori(1 if l == 0 else 0, 4) as i:
                    for s in range(3):
                        sp.wait_ge(mod_mm, 12 * l + 3 * i + s - 2)
                        block(l, 3 * i + s, s)

        def inputs_pe(pe):
            pe.wait_ge(consts_in, CONST_DMAS)
            pe.wait_ge(params_in, 16 * 15)
            for q, n in enumerate(NROWS):
                nc.tensor.transpose(PS[:, 4 + q, 0:n], ROWS4[0:n, q, :],
                                    ident[0:n, 0:n]).then_inc(params_T, 1)
            pe.wait_ge(c_silu, 1)
            pe.wait_ge(params_ready, 4)

            def cols(i, s):
                pe.wait_ge(mod_row, 3 * i + s + 1)
                pe.wait_ge(mod_added, 3 * i + s + 1)
                pe.sem_inc(passed, 1)
                for q in range(4):
                    last = nc.tensor.transpose(PS[:, 3 + s, 2 * q:2 * q + 2], MROW[0:2, s, 128 * q:128 * q + 128],
                                               ident[0:2, 0:2])
                last.then_inc(mod_cols, 1)

            with pe.Fori(0, 8) as i:
                for s in range(3):
                    pe.wait_ge(mod_full[s], 16 * i + 16)
                    for k in range(CT):
                        last = nc.tensor.matmul(PS[0:2, s, :], CS[:, k:k + 9:8], MW[:, s, k, :],
                                                start=k == 0, stop=k == CT - 1)
                    last.then_inc(mod_mm, 1)
                    if s:
                        cols(i, s - 1)
                cols(i, 2)
            pe.wait_ge(x_in, 32)
            for c in range(CT):
                b = 2 * (c % 3)
                pe.wait_ge(mod_added, 27)
                if c >= 3:
                    pe.wait_ge(x_evicted, c - 2)
                for k in range(6):
                    last = nc.tensor.transpose(PS[:, b + k // 3, 128 * (k % 3):128 * (k % 3) + 128],
                                               XT[:, k, 128 * c:128 * c + 128], ident[:, :])
                last.then_inc(x_T, 1)

        def inputs_act(act):
            act.wait_ge(params_ready, 1)
            nc.scalar.activation(CS, PC[:, 0:16], ACT.Silu).then_inc(c_silu, 1)
            with act.Fori(0, 8) as i:
                for s in range(3):
                    act.wait_ge(mod_mm, 3 * i + s + 1)
                    nc.scalar.activation(MROW[0:2, s, :], PS[0:2, s, :], ACT.Copy).then_inc(mod_row, 1)
            for c in range(CT):
                act.wait_ge(x_T, c + 1)
                nc.scalar.activation(as_halves(X[:, c, :]), halves(2 * (c % 3)), ACT.Copy).then_inc(x_evicted, 1)

        def inputs_dve(v):
            v.sem_inc(mod_added, 3)
            nc.vector.memset(small[:, 0:1], EPS).then_inc(consts_set, 1)
            nc.vector.memset(small[:, 1:2], -1.0).then_inc(consts_set, 1)
            nc.vector.memset(small[:, 3:4], GN_EPS).then_inc(consts_set, 1)
            for q, n in enumerate(NROWS):
                v.wait_ge(params_T, q + 1)
                nc.vector.tensor_copy(PC[:, PBASE[q]:PBASE[q] + n], PS[:, 4 + q, 0:n])\
                  .then_inc(params_ready, 1)
            v.wait_ge(params_ready, 4)
            mt = modT[:, :, :, :].rearrange("p l j w -> p (l j) w")
            with v.Fori(0, 8) as i:
                for s in range(3):
                    v.wait_ge(mod_cols, 3 * i + s + 1)
                    b = PC[:, bass.ds(PBASE[1] + 12 * i + 4 * s, 4)].unsqueeze(2).broadcast_to([128, 4, 2])
                    nc.vector.tensor_tensor(mt[:, bass.ds(12 * i + 4 * s, 4), :],
                                            PS[:, 3 + s, 0:8].rearrange("p (q w) -> p q w", w=2), b, ALU.add)\
                      .then_inc(mod_added, 1)
            v.wait_ge(mod_added, 27)
            for l in range(2):
                for w in range(2):
                    for k in range(4):
                        m = modT[:, l, 8 * (1, 2, 4, 5)[k]:8 * (1, 2, 4, 5)[k] + 8, w]
                        g = PC[:, G_COL(l, k, 0):G_COL(l, k, 0) + 8]
                        last = nc.vector.scalar_tensor_tensor(DER[:, l, k, w, :], m, 1.0 if k % 2 == 0 else 0.0, g,
                                                              ALU.add, ALU.mult)
            last.then_inc(gains_ready, 1)

        consts_set = sem("consts_set")

        def output_pe(pe, updates):
            pe.wait_ge(x_updated, updates)
            for k in range(4):
                if k >= 3:
                    pe.wait_ge(out_sb, 2 * k - 4)
                for c in range(CT):
                    last = nc.tensor.transpose(PS[:, 2 * (k % 3) + 2 + c // 4, 128 * (c % 4):128 * (c % 4) + 128],
                                               X[:, c, 128 * k:128 * k + 128], ident[:, :])
                    if c % 4 == 3:
                        last.then_inc(out_T, 1)

        def output_act(act):
            for k in range(4):
                for h in range(2):
                    act.wait_ge(out_T, 2 * k + h + 1)
                    nc.scalar.activation(Yf[:, 1024 * k + 512 * h:1024 * k + 512 * h + 512],
                                         PS[:, 2 * (k % 3) + 2 + h, :], ACT.Copy).then_inc(out_sb, 1)

        def output_sp(sp):
            for k in range(4):
                sp.wait_ge(out_sb, 2 * k + 2)
                sp.dma_start(out[0, 128 * k:128 * k + 128, :], Yf[:, 1024 * k:1024 * k + 1024]).then_inc(stored, 16)
            sp.wait_ge(stored, 64)

        Hf = lambda t, s0, s1: H[:, t, s0:s1]
        inproj = Dense("inproj", "plain", 6, 0, a["mix_w_in"][0], lambda k: H[:, k, :], P)
        outproj = Dense("outproj", "plain", 2, 6, a["mix_w_out"][0], lambda k: H[:, k, :], Y)
        gate0 = Dense("gate0", "gate", 11, 8, (a["ffn_w1"][0], a["ffn_w3"][0]), lambda k: H[:, k, :], P)
        down0 = Dense("down0", "long", 4, 19, a["ffn_w2"][0], lambda k: P[:, k, :], Y)


        def padded(t, s0, s1, shift=0):
            at = s0 + (1 if s0 < L else 2) + shift
            return Hpad[:, t, at:at + s1 - s0]

        XX = Y
        MIX = (P[:, 16:24, :], TMP[:, 0:CT * T].rearrange("p (c t) -> p c t", c=CT))
        TH, AH, GH, GH2, W2S, A2S, G2S, G2S2, HONES, PCS, STATE, ENDS = carve(
            TMP[:, CT * T:TMPN], [T, T, L, L, 128, 128, 128, 128, 128, 10, 128, 24])
        MIXES = (5, 1, 4, 3, 2, 0)
        LORA = 23
        GR = GLORA - 128
        pads_set = sem("pads_set")
        back_in = sem("back_in")
        xx_ready = sem("xx_ready")
        mix_ready = sem("mix_ready")
        lora_hid = sem("lora_hid")
        gate_hid = sem("gate_hid")
        value = Dense("value", "plain", 2, 24, a["rw_w_rkv"][0, 2], lambda k: MIX[1][:, k, :], P[:, 8:16, :])
        key = Dense("key", "plain", 2, 26, a["rw_w_rkv"][0, 1], lambda k: MIX[0][:, k, :], P[:, 0:8, :])
        recept = Dense("recept", "plain", 2, 28, a["rw_w_rkv"][0, 0], lambda k: MIX[1][:, k, :], P[:, 16:24, :], L)

        def mixes_sp(sp):
            g1 = a["rw_g1"][0].rearrange("(k p) r -> p k r", p=128)
            parts = [(0, WR[:, 0, 0:CT, :], g1[:, :, 0:128], w_full[0]),
                     (1, WR[:, 1, 0:CT, 0:GR], g1[:, :, 128:GLORA], w_full[1])]
            for s, name in ((2, "rw_w1"), (3, "rw_a1")):
                for e in range(2):
                    parts.append((s, WR[:, s, 0:CT, 64 * e:64 * e + 64],
                                  a[name][0, e].rearrange("(k p) r -> p k r", p=128), (w_full[s], back_in)[e]))
            for s, dst, src, signal in parts:
                sp.wait_ge(slots_used, 4 * (LORA - 1) + s + 1)
                sp.dma_start(dst, src).then_inc(signal, 16)

        def mixes_pe(pe):
            jobs = ((0, MIX[0], 128, L), (1, MIX[0], GR, L), (2, MIX[1], 128, T), (3, MIX[0], 128, T))
            for s, x, m, n in jobs:
                pe.wait_ge(mix_ready, 8 * max(s, 1))
                pe.wait_ge(w_full[s], 16 * (LORA + 1))
                if s >= 2:
                    pe.wait_ge(back_in, 32)
                for k in range(CT):
                    for h0, h1, b in (((0, HALF, 0), (HALF, T, 1)) if n == T else ((0, L, 0),)):
                        last = nc.tensor.matmul(PS[0:m, 2 * s + b, 0:h1 - h0], WR[:, s, k, 0:m], x[:, k, h0:h1],
                                                start=k == 0, stop=k == CT - 1)
                last.then_inc(slots_used, 1)

        def mixes_act(act):
            u = 4 * LORA
            act.wait_ge(slots_used, u + 1)
            nc.scalar.activation(GH, PS[:, 0, 0:L], ACT.Tanh, scale=0.5).then_inc(lora_hid, 1)
            act.wait_ge(slots_used, u + 2)
            nc.scalar.activation(GH2[0:GR, :], PS[0:GR, 2, 0:L], ACT.Tanh, scale=0.5).then_inc(lora_hid, 1)
            act.wait_ge(slots_used, u + 3)
            nc.scalar.activation(as_halves(TH), halves(4), ACT.Tanh).then_inc(lora_hid, 1)
            act.wait_ge(slots_used, u + 4)
            nc.scalar.activation(as_halves(AH), halves(6), ACT.Copy).then_inc(lora_hid, 1)

        def mixes_dve(v):
            v.wait_ge(pads_set, 3)
            for t in range(CT):
                v.wait_ge(normed, NORMED_BASE[4] + t + 1)
                for s0, s1, _ in segs():
                    ins = nc.vector.tensor_tensor(XX[:, t, s0:s1], padded(t, s0, s1, -1), padded(t, s0, s1, 1), ALU.add)
                ins.then_inc(xx_ready, 1)
                v.wait_ge(xx_ready, 2 * t + 1)
                for s0, s1, _ in segs():
                    ins = nc.vector.scalar_tensor_tensor(XX[:, t, s0:s1], XX[:, t, s0:s1], 0.5, padded(t, s0, s1),
                                                         ALU.mult, ALU.subtract)
                ins.then_inc(xx_ready, 1)
            v.wait_ge(xx_ready, 2 * CT)
            used = {2: 4 * LORA + 2, 3: 4 * LORA + 3, 4: 4 * LORA + 4, 5: 4 * value.base + 8}
            for n, mu in enumerate(MIXES):
                if n in used:
                    v.wait_ge(slots_used, used[n])
                if n == 2:
                    v.wait_ge(lora_hid, 2)
                    nc.vector.tensor_scalar(GH, GH, 0.5, 0.5, ALU.mult, ALU.add).then_inc(gate_hid, 1)
                    nc.vector.tensor_scalar(GH2[0:GR, :], GH2[0:GR, :], 0.5, 0.5, ALU.mult, ALU.add)\
                      .then_inc(gate_hid, 1)
                for t in range(CT):
                    for s0, s1, _ in segs(L if mu in (0, 5) else T):
                        ins = nc.vector.scalar_tensor_tensor(MIX[n % 2][:, t, s0:s1], XX[:, t, s0:s1],
                                                             col(MU_COL + 8 * mu + t), padded(t, s0, s1),
                                                             ALU.mult, ALU.add)
                    ins.then_inc(mix_ready, 1)

        TC = 64
        NCH = T // TC
        NLAT = L // TC
        NX = NCH
        BK = 16
        NBLK = NX * 2 * (TC // BK)
        DEC0 = math.exp(-0.5)
        KPR, XY, LV, ZERO = carve(Hraw, [2 * (T + L), 48 * TC, 4 * TC, 128])
        KPR = KPR.rearrange("p (e t) -> p e t", e=2)
        XY = XY.rearrange("p (a x t) -> p a x t", a=4, t=TC)
        LV = LV.rearrange("p (l d t) -> p l d t", l=2, d=2)
        Xs = X[:, :, :].rearrange("p c t -> p (c t)")
        GAB, GCD, WI0 = carve(Xs, [2 * 2 * NX * TC, 2 * 2 * 8 * TC, T])
        GAB = GAB.rearrange("p (a e x t) -> p a e x t", a=2, e=2, t=TC)
        GCD = GCD.rearrange("p (a e x t) -> p a e x t", a=2, e=2, t=TC)
        TOK, VTT, VS, MK, RUN = carve(WRf, [4 * T, T, T, 4 * TC, T])
        TOK = TOK.rearrange("p (e w j c) -> p e w j c", e=2, w=2, j=6)
        VTT = VTT.rearrange("p (j c) -> p j c", j=6)
        MK = MK.rearrange("p (e a t) -> p e a t", e=2, a=2)
        SG, SUMS, EP, EN, AA, BT, KT, KK = carve(TMP[:, 0:8 * T], [T] * 8)
        BLK, YB, PROD, XB = SG[0:NBLK, 0:512], SUMS[0:NBLK, 0:512], EN[0:NBLK, 0:512], AA[0:NBLK, 0:512]
        Z = Yf[:, 0:CT * L].rearrange("p (c t) -> p c t", c=CT)
        WI1, YS, RHS, NSA, FIN = carve(Yf[:, CT * L:CT * T], [T, L, 128, 128, L])
        WI = [w.rearrange("p (x t) -> p x t", t=TC) for w in (WI0, WI1)]
        BV = [w.rearrange("p (x t) -> p x t", t=TC) for w in (KK, EP)]
        ACC = P[:, 16:18, L:T]
        STATE = STATE.rearrange("p (e v) -> p e v", e=2)
        ENDS = ENDS.rearrange("p (e j) -> p e j", e=2)
        PW0, PA0, PKK, PKA, PRK, PLW, PLB = 0, 2, 4, 5, 6, 8, 9
        x_keep = nc.dram_tensor("x_keep", (128, CT, L), F32, kind="Internal").ap()
        blk_dram = nc.dram_tensor("blk_dram", (2, NX, 2, 4, BK, BK), F32, kind="Internal").ap()
        inv_dram = nc.dram_tensor("inv_dram", (4, NX, 2, 4, BK, BK), F32, kind="Internal").ap()

        x_kept = sem("x_kept")
        x_back = sem("x_back")
        scan_in = sem("scan_in")
        scan_set = sem("scan_set")
        lora2_in = sem("lora2_in")
        cols_halved = sem("cols_halved")
        turn_in = sem("turn_in")
        xy_zero = sem("xy_zero")
        lora_mm = sem("lora_mm")
        tanh_ready = sem("tanh_ready")
        sig_ready = sem("sig_ready")
        cs_ready = sem("cs_ready")
        decay_ready = sem("decay_ready")
        kk_raw = sem("kk_raw")
        kk_mm = sem("kk_mm")
        kk_root = sem("kk_root")
        feat_ready = sem("feat_ready")
        gram_mm = sem("gram_mm")
        g_ready = sem("g_ready")
        tok_mm = sem("tok_mm")
        tok_ready = sem("tok_ready")
        blk_out = sem("blk_out")
        blk_back = sem("blk_back")
        sub_step = sem("sub_step")
        inv16_ready = sem("inv16_ready")
        inv16_out = sem("inv16_out")
        xy_in = sem("xy_in")
        inv_w = sem("inv_w")
        w_ready = sem("w_ready")
        inv_xy = sem("inv_xy")
        xy_ready = sem("xy_ready")
        bv_mm = sem("bv_mm")
        bv_ready = sem("bv_ready")
        y_cleared = sem("y_cleared")
        rh_mm = sem("rh_mm")
        rh_ready = sem("rh_ready")
        sa_mm = sem("sa_mm")
        sa_ready = sem("sa_ready")
        st_mm = sem("st_mm")
        st_ready = [sem("st_ready_f"), sem("st_ready_b")]
        y_mm = sem("y_mm")
        y_out = sem("y_out")
        cg_mm = sem("cg_mm")
        mean_mm = sem("mean_mm")
        centred = sem("centred")
        sq_done = sem("sq_done")
        var_mm = sem("var_mm")
        gn_root = sem("gn_root")
        z_out = sem("z_out")
        scan_step = sem("scan_step")

        def order(e):
            c, l = list(range(NLAT, NCH)), list(range(NLAT))
            return c + l if e == 0 else c[::-1] + l[::-1]

        def strided(ap, *dims):
            return bass.AP(ap.tensor, ap.offset, [list(ap.ap[0])] + [list(d) for d in dims])

        def scan_sp(sp):
            sp.wait_ge(normed, NORMED_BASE[4] + CT)
            sp.dma_start(x_keep, X[:, :, 0:L]).then_inc(x_kept, 16)
            sp.wait_ge(slots_used, 4 * recept.base + 8)
            for dst, src in ((MK, a["grammask"]), (LV, a["levelmask"]), (RUN, a["run"]), (HONES, a["headones"])):
                sp.dma_start(dst, src).then_inc(scan_in, 16)
            with sp.Fori(0, CT) as i:
                sp.wait_ge(z_out, i + 1)
                for dst, src in ((W2S, a["rw_w2"][0].rearrange("e r (c d) -> c (e r) d", d=128)),
                                 (A2S, a["rw_a2"][0].rearrange("e r (c d) -> c (e r) d", d=128)),
                                 (G2S, a["rw_g2"][0, 0:128, :].rearrange("r (c d) -> c r d", d=128)),
                                 (G2S2[0:GR, :], a["rw_g2"][0, 128:GLORA, :].rearrange("r (c d) -> c r d", d=128))):
                    sp.dma_start(dst, src[bass.ds(i, 1)].rearrange("a r d -> (a r) d")).then_inc(lora2_in, 16)
                sp.wait_ge(g_ready, 24 * i + 24)
                for p in range(2):
                    for b in range(4):
                        at = 64 * p + BK * b
                        sp.dma_start(blk_dram[:, :, p, b].rearrange("e x s t -> s (e x) t"),
                                     GAB[at:at + BK, 0, :, :, BK * b:BK * b + BK].rearrange("s e x t -> s (e x) t"))\
                          .then_inc(blk_out, 16)
                sp.wait_ge(blk_out, 128 * i + 128)
                sp.dma_start(BLK.rearrange("q (e n) -> q e n", e=2),
                             blk_dram.rearrange("e x p b s t -> (x p b) e (s t)")).then_inc(blk_back, 16)
                for k, src in ((2, YB), (0, XB)):
                    sp.wait_ge(inv16_ready, 2 * i + (1 if k else 2))
                    sp.dma_start(inv_dram[k:k + 2].rearrange("e x p b s t -> (x p b) e (s t)"),
                                 src.rearrange("q (e n) -> q e n", e=2)).then_inc(inv16_out, 16)
                sp.wait_ge(inv16_out, 32 * i + 32)
                sp.wait_ge(xy_zero, i + 1)
                for p in range(2):
                    for b in range(4):
                        at = 64 * p + BK * b
                        sp.dma_start(XY[at:at + BK, :, :, BK * b:BK * b + BK].rearrange("s a x t -> s (a x) t"),
                                     inv_dram[:, :, p, b].rearrange("a x s t -> s (a x) t")).then_inc(xy_in, 16)
            sp.wait_ge(z_out, CT + 1)
            sp.wait_ge(x_kept, 16)
            sp.dma_start(X[:, :, 0:L], x_keep).then_inc(x_back, 16)

        def scan_pool(pool):
            pool.wait_ge(cols_halved, 1)
            pool.wait_ge(recept.unit_free, recept.done)
            pool.wait_ge(slots_used, 4 * recept.base + 8)
            nc.gpsimd.memset(ZERO[0:1, :], 0.0).then_inc(scan_set, 1)
            pc = PC[:, PBASE[3]:PBASE[3] + 80].rearrange("p (g c) -> p g c", c=8)
            with pool.Fori(0, CT) as i:
                pool.wait_ge(z_out, i + 1)
                nc.gpsimd.tensor_copy(PCS.unsqueeze(2), pc[:, :, bass.ds(i, 1)]).then_inc(turn_in, 1)
                nc.gpsimd.tensor_copy(VS, P[:, bass.ds(8 + i, 1), :].rearrange("p a t -> p (a t)")).then_inc(turn_in, 1)

                def sigmoid(e, k):
                    pool.wait_ge(tanh_ready, 4 * i + 2 * e + k + 1)
                    pool.sem_inc(passed, 1)
                    x = (SG, AA)[k]
                    nc.gpsimd.tensor_scalar(x, x, 0.5, 0.5, ALU.mult, ALU.add).then_inc(sig_ready, 1)
                sigmoid(0, 0)
                sigmoid(0, 1)
                nc.gpsimd.memset(XY[:, :, :, :].rearrange("p a x t -> p (a x t)"), 0.0).then_inc(xy_zero, 1)
                sigmoid(1, 0)
                sigmoid(1, 1)

        def scan_pe(pe):
            def tokens(i, n, src):
                pe.wait_ge(tok_ready, 5 * i + n + 1)
                for k in range(6):
                    last = nc.tensor.transpose(PS[:, 6 + k // 3, 128 * (k % 3):128 * (k % 3) + 128],
                                               src[:, 128 * k:128 * k + 128], ident[:, :])
                last.then_inc(tok_mm, 1)

            def lora(i, e, k, bank):
                r = slice(64 * e, 64 * e + 64)
                w, x = ((W2S, TH), (A2S, AH))[k]
                for h in range(2):
                    last = nc.tensor.matmul(PS[:, bank + h, 0:HALF], w[r, :], x[r, HALF * h:HALF * h + HALF],
                                            start=True, stop=True)
                last.then_inc(lora_mm, 1)

            def products(i, e):
                pe.wait_ge(feat_ready, 2 * i + e + 1)
                if e:
                    pe.wait_ge(g_ready, 24 * i + 12)
                pe.sem_inc(passed, 1)
                for q in range(3):
                    for h in range(2):
                        hr = slice(64 * h, 64 * h + 64)
                        for j in (2 * q, 2 * q + 1):
                            for p in range(2):
                                ch = 2 * j + p
                                pr = slice(64 * p, 64 * p + 64)
                                n = 128 if j < 4 else 64
                                moving = KPR[hr, e, 64 * ch:64 * ch + 64]
                                if j < 4:
                                    moving = strided(moving, (T, 2), (1, 64))
                                for w, x in ((0, BT), (1, KT)):
                                    at = 2 * n * (j % 2) + n * w
                                    last = nc.tensor.matmul(PS[pr, q + 3 * h, at:at + n], x[hr, 64 * ch:64 * ch + 64],
                                                            moving, start=True, stop=True)
                        last.then_inc(gram_mm, 1)

            def all_products(bank, lhs, rhs):
                for x in range(NX):
                    for p in range(2):
                        pr = slice(64 * p, 64 * p + 64)
                        last = nc.tensor.matmul(PS[pr, bank + x // 6, 64 * (x % 6):64 * (x % 6) + 64],
                                                lhs(x, pr), rhs(x, pr), start=True, stop=True)
                return last

            def inverses(i):
                at = lambda e: (lambda x, pr: GAB[pr, 0, e, x, :])
                xi = lambda e: (lambda x, pr: XY[pr, e, x, :])
                yi = lambda e: (lambda x, pr: XY[pr, 2 + e, x, :])
                wi = lambda e: (lambda x, pr: WI[e][pr, x, :])
                pe.wait_ge(g_ready, 24 * i + 24)
                pe.sem_inc(passed, 1)
                bt = lambda e: (lambda x, pr: GAB[pr, 1, e, x, :])
                vt = lambda x, pr: VTT[pr, x // 2, 64 * (x % 2):64 * (x % 2) + 64]
                all_products(0, bt(0), vt).then_inc(bv_mm, 1)
                all_products(2, bt(1), vt).then_inc(bv_mm, 1)
                pe.wait_ge(xy_in, 128 * i + 128)
                pe.wait_ge(tok_ready, 5 * i + 6)
                pe.wait_ge(bv_ready, 2 * i + 2)
                pe.sem_inc(passed, 1)
                all_products(0, at(0), xi(0)).then_inc(inv_w, 1)
                all_products(2, at(1), xi(1)).then_inc(inv_w, 1)
                pe.wait_ge(w_ready, 4 * i + 1)
                pe.sem_inc(passed, 1)
                all_products(4, yi(0), wi(0))
                all_products(6, wi(0), yi(0)).then_inc(inv_xy, 1)
                pe.wait_ge(w_ready, 4 * i + 2)
                pe.sem_inc(passed, 1)
                all_products(0, yi(1), wi(1))
                all_products(2, wi(1), yi(1)).then_inc(inv_xy, 1)
                pe.wait_ge(xy_ready, 4 * i + 1)
                pe.sem_inc(passed, 1)
                all_products(4, at(0), xi(0)).then_inc(inv_w, 1)
                pe.wait_ge(xy_ready, 4 * i + 2)
                pe.sem_inc(passed, 1)
                all_products(0, at(1), xi(1)).then_inc(inv_w, 1)
                pe.wait_ge(w_ready, 4 * i + 3)
                pe.sem_inc(passed, 1)
                all_products(6, wi(0), yi(0)).then_inc(inv_xy, 1)
                pe.wait_ge(w_ready, 4 * i + 4)
                pe.sem_inc(passed, 1)
                all_products(2, wi(1), yi(1)).then_inc(inv_xy, 1)
                pe.wait_ge(xy_ready, 4 * i + 4)
                pe.sem_inc(passed, 1)
                for b in (5, 6, 7):
                    last = nc.tensor.matmul(PS[:, b, 0:TC], ZERO[0:1, :], RUN[0:1, 0:TC], start=True, stop=True)
                last.then_inc(y_cleared, 1)

            def add(out, lhs, rhs):
                return nc.tensor.matmul(out, lhs, rhs, start=False, stop=True, skip_group_check=True)

            def chunks(i):
                pe.wait_ge(y_cleared, i + 1)
                H2 = [slice(0, 64), slice(64, 128)]
                for n in range(NCH):
                    both = [(e, order(e)[n], H2[order(e)[n] % 2]) for e in range(2)]
                    latent = n >= NCH - NLAT
                    for e, ch, pr in both:
                        pe.wait_ge(st_ready[e], 13 * i + n + 1)
                        pe.sem_inc(passed, 1)
                        for h, hr in enumerate(H2):
                            last = nc.tensor.matmul(PS[pr, h, 0:64], KPR[hr, e, 64 * ch:64 * ch + 64], STATE[hr, e, :],
                                                    start=True, stop=True)
                        last.then_inc(rh_mm, 1)
                    if latent:
                        for e, ch, pr in both:
                            for hr in H2:
                                add(PS[hr, 5, 64 * ch:64 * ch + 64], STATE[hr, e, :],
                                    KPR[hr, e, T + 64 * ch:T + 64 * ch + 64])
                    for e, ch, pr in both:
                        pe.wait_ge(rh_ready, 24 * i + 2 * n + e + 1)
                        pe.sem_inc(passed, 1)
                        for h, hr in enumerate(H2):
                            last = nc.tensor.matmul(PS[pr, 2, hr], XY[pr, 2 + e, 2 * (ch // 2) + h, :], RHS[pr, hr],
                                                    start=True, stop=True)
                        last.then_inc(sa_mm, 1)
                    for e, ch, pr in both:
                        j = ch // 2
                        pe.wait_ge(sa_ready, 24 * i + 2 * n + e + 1)
                        pe.sem_inc(passed, 1)
                        for hr in H2:
                            nc.tensor.matmul(PS[hr, 3 + e, 0:64], TOK[pr, e, 0, j, hr], NSA[pr, hr],
                                             start=True, stop=False)
                            last = nc.tensor.matmul(PS[hr, 3 + e, 0:64], TOK[pr, e, 1, j, hr], VTT[pr, j, hr],
                                                    start=False, stop=True)
                        last.then_inc(st_mm, 1)
                    if latent:
                        for e, ch, pr in both:
                            j = ch // 2
                            for h, hr in enumerate(H2):
                                out = PS[hr, 6 + ch % 2, 64 * ch:64 * ch + 64]
                                add(out, VTT[pr, j, hr], GCD[pr, 1, e, 2 * j + h, :])
                                last = add(out, NSA[pr, hr], GCD[pr, 0, e, 2 * j + h, :])
                last.then_inc(y_mm, 1)

            pe.wait_ge(scan_set, 1)
            with pe.Fori(0, CT) as i:
                pe.wait_ge(z_out, i + 1)
                pe.wait_ge(turn_in, 2 * i + 2)
                tokens(i, 0, VS)
                pe.wait_ge(kk_raw, 2 * i + 2)
                pe.sem_inc(passed, 1)
                for h in range(2):
                    last = nc.tensor.matmul(PS[:, 4 + h, 0:HALF], HONES, BT[:, HALF * h:HALF * h + HALF],
                                            start=True, stop=True)
                last.then_inc(kk_mm, 1)
                pe.wait_ge(lora2_in, 64 * i + 64)
                pe.sem_inc(passed, 1)
                lora(i, 0, 0, 0)
                lora(i, 0, 1, 2)
                pe.wait_ge(tok_ready, 5 * i + 2)
                pe.sem_inc(passed, 1)
                lora(i, 1, 0, 6)
                products(i, 0)
                pe.wait_ge(tanh_ready, 4 * i + 3)
                tokens(i, 1, BT)
                tokens(i, 2, KT)
                pe.wait_ge(tok_ready, 5 * i + 4)
                pe.sem_inc(passed, 1)
                lora(i, 1, 1, 6)
                products(i, 1)
                tokens(i, 3, BT)
                tokens(i, 4, KT)
                inverses(i)
                chunks(i)
                pe.wait_ge(y_out, i + 1)
                pe.sem_inc(passed, 1)
                nc.tensor.matmul(PS[:, 0, 0:L], HONES, YS, start=True, stop=True).then_inc(mean_mm, 1)
                nc.tensor.matmul(PS[:, 2, 0:L].rearrange("p (a t) -> p a t", a=2), HONES, ACC, start=True, stop=True)
                nc.tensor.matmul(PS[:, 3, 0:L], G2S, GH, start=True, stop=False)
                nc.tensor.matmul(PS[:, 3, 0:L], G2S2[0:GR, :], GH2[0:GR, :], start=False, stop=True).then_inc(cg_mm, 1)
                pe.wait_ge(sq_done, i + 1)
                pe.sem_inc(passed, 1)
                nc.tensor.matmul(PS[:, 1, 0:L], HONES, FIN, start=True, stop=True).then_inc(var_mm, 1)

        def scan_act(act):
            def evict_tokens(i, n, dst):
                act.wait_ge(tok_mm, 5 * i + n + 1)
                nc.scalar.activation(dst.rearrange("p (g k) c -> p g k c", g=2),
                                     halves(6).rearrange("p g (k c) -> p g k c", k=3), ACT.Copy).then_inc(tok_ready, 1)

            def tangent(i, e, k, bank):
                act.wait_ge(lora_mm, 4 * i + 2 * e + k + 1)
                w = (PW0, PA0)[k] + e
                nc.scalar.activation(as_halves((SG, AA)[k]), halves(bank), ACT.Tanh, scale=0.5,
                                     bias=PCS[:, w:w + 1]).then_inc(tanh_ready, 1)

            def decays(i, e):
                act.wait_ge(cs_ready, 2 * i + e + 1)
                nc.scalar.activation(EP, SUMS, ACT.Exp, scale=-DEC0)
                nc.scalar.activation(EN, SUMS, ACT.Exp, scale=DEC0).then_inc(decay_ready, 1)

            act.sem_inc(tok_ready, 1)
            with act.Fori(0, CT) as i:
                act.wait_ge(turn_in, 2 * i + 2)
                act.wait_ge(z_out, i + 1)
                act.sem_inc(passed, 1)
                nc.scalar.activation(KK, P[:, bass.ds(i, 1), :].rearrange("p a t -> p (a t)"), ACT.Copy,
                                     scale=PCS[:, PKK:PKK + 1]).then_inc(kk_raw, 1)
                act.wait_ge(kk_raw, 2 * i + 1)
                nc.scalar.activation(BT, KK, ACT.Square).then_inc(kk_raw, 1)
                act.wait_ge(kk_mm, i + 1)
                nc.scalar.activation(as_halves(KT), halves(4), ACT.Sqrt).then_inc(kk_root, 1)
                evict_tokens(i, 0, VTT[:, :, :])
                tangent(i, 0, 0, 0)
                tangent(i, 0, 1, 2)
                decays(i, 0)
                tangent(i, 1, 0, 6)
                evict_tokens(i, 1, TOK[:, 0, 0])
                evict_tokens(i, 2, TOK[:, 0, 1])
                tangent(i, 1, 1, 6)
                decays(i, 1)
                evict_tokens(i, 3, TOK[:, 1, 0])
                evict_tokens(i, 4, TOK[:, 1, 1])
                for e, bank in ((0, 0), (1, 2)):
                    act.wait_ge(bv_mm, 2 * i + e + 1)
                    nc.scalar.activation(BV[e][:, :, :].rearrange("p (b x) t -> p b x t", b=2),
                                         PS[:, bank:bank + 2, 0:HALF].rearrange("p b (x t) -> p b x t", t=TC), ACT.Copy)\
                      .then_inc(bv_ready, 1)
                for n in range(NCH):
                    for e in range(2):
                        p = order(e)[n] % 2
                        pr = slice(64 * p, 64 * p + 64)
                        act.wait_ge(sa_mm, 24 * i + 2 * n + e + 1)
                        nc.scalar.activation(NSA[pr, :], PS[pr, 2, 0:128], ACT.Copy, scale=-1.0).then_inc(sa_ready, 1)
                act.wait_ge(centred, i + 1)
                nc.scalar.activation(FIN, YS, ACT.Square).then_inc(sq_done, 1)
                act.wait_ge(var_mm, i + 1)
                nc.scalar.activation(FIN, PS[:, 1, 0:L], ACT.Sqrt, scale=1.0 / CH, bias=small[:, 3:4]).then_inc(gn_root, 1)

        SCAN_LINKS = 3 + 2 * 4 + 1 + 2 * NCH + 1 + 5
        SUB_LINKS = 1 + 2 * (BK - 1)

        def scan_dve(v):
            v.sem_inc(z_out, 1)
            nc.vector.tensor_scalar(PC[:, W0_COL:W0_COL + 32], PC[:, W0_COL:W0_COL + 32], 0.5, None, ALU.mult)\
              .then_inc(cols_halved, 1)
            chain = Chain(v, scan_step, SCAN_LINKS)
            sub = Chain(v, sub_step, SUB_LINKS)
            v.wait_ge(scan_in, 16 * 4)
            v.wait_ge(x_kept, 16)
            v.wait_ge(recept.unit_free, recept.done)

            def features(e, i):
                u = 2 * i + e
                kdyn = P[:, bass.ds(i, 1), :].rearrange("p a t -> p (a t)")
                rdyn = P[:, bass.ds(16 + i, 1), 0:L].rearrange("p a t -> p (a t)")
                chunked = lambda x: x.rearrange("p (j t) -> p j t", t=TC)
                v.wait_ge(sig_ready, 4 * i + 2 * e + 1)
                nc.vector.memset(STATE[:, e, :], 0.0).then_inc(st_ready[e], 1)
                flip = (lambda x: x) if e == 0 else (lambda x: x[:, ::-1])
                nc.vector.tensor_tensor_scan(flip(SUMS), RUN, flip(SG), 0.0, ALU.mult, ALU.add).then_inc(cs_ready, 1)
                if e == 0:
                    v.wait_ge(kk_root, i + 1)
                    chain.link(nc.vector.tensor_scalar(KT, KT, 1e-12, None, ALU.max))
                    chain.link(nc.vector.reciprocal(KT, KT))
                    chain.link(nc.vector.tensor_tensor(KK, KK, KT, ALU.mult))
                v.wait_ge(decay_ready, u + 1)
                v.wait_ge(sig_ready, 4 * i + 2 * e + 2)
                if e == 1:
                    v.wait_ge(tok_mm, 5 * i + 3)
                chain.link(nc.vector.tensor_tensor(BT, KK, AA, ALU.mult))
                nc.vector.tensor_tensor(BT, BT, EN, ALU.mult)
                kin, kc, ec = chunked(KPR[:, e, 0:T]), chunked(KK), chunked(EP)
                last, now, before, first = ((TC - 1, slice(1, TC), slice(0, TC - 1), 0) if e == 0 else
                                            (0, slice(0, TC - 1), slice(1, TC), TC - 1))
                nc.vector.tensor_tensor(kin[:, :, now], kc[:, :, now], ec[:, :, before], ALU.mult)
                nc.vector.tensor_copy(kin[:, :, first:first + 1], kc[:, :, first:first + 1])
                nc.vector.tensor_copy(ENDS[:, e, :].unsqueeze(2), ec[:, :, last:last + 1])
                nc.vector.tensor_tensor(KPR[:, e, T:T + L], rdyn, EP[:, 0:L], ALU.mult)
                chain.link(nc.vector.tensor_scalar(AA, AA, 1.0, PCS[:, PKA:PKA + 1], ALU.subtract, ALU.mult))
                chain.link(nc.vector.scalar_tensor_tensor(SUMS, AA, 1.0, kdyn, ALU.add, ALU.mult))
                nc.vector.tensor_tensor(KT, SUMS, EN, ALU.mult).then_inc(feat_ready, 1)
                kd = SUMS[:, 0:L].rearrange("p (a t) -> p a t", a=2)
                if e == 0:
                    chain.link(nc.vector.tensor_scalar(ACC, kd, PCS[:, PRK:PRK + 1], None, ALU.mult))
                else:
                    chain.link(nc.vector.scalar_tensor_tensor(ACC, kd, PCS[:, PRK + 1:PRK + 2], ACC,
                                                              ALU.mult, ALU.add))
                    chain.link(nc.vector.tensor_tensor(ACC, ACC, rdyn.rearrange("p (a t) -> p a t", a=2), ALU.mult))

            def masked(e, i):
                for q in range(3):
                    for h in range(2):
                        v.wait_ge(gram_mm, 12 * i + 6 * e + 2 * q + h + 1)
                        x = slice(4 * q + h, 4 * q + 4, 2)
                        if q < 2:
                            ps = PS[:, q + 3 * h, :].rearrange("p (j w a t) -> p a w j t", j=2, w=2, a=2)
                            for k, g in enumerate((GAB, GCD)):
                                nc.vector.tensor_tensor(g[:, :, e, x, :], MK[:, e, k:k + 1, :].unsqueeze(1)
                                                        .broadcast_to([128, 2, 2, TC]), ps[:, k], ALU.mult)\
                                  .then_inc(g_ready, 1)
                        else:
                            ps = PS[:, q + 3 * h, 0:256].rearrange("p (j w t) -> p w j t", j=2, w=2)
                            nc.vector.tensor_tensor(GAB[:, :, e, x, :], MK[:, e, 0:1, :].unsqueeze(1)
                                                    .broadcast_to([128, 2, 2, TC]), ps, ALU.mult).then_inc(g_ready, 2)

            def substitution(i):
                sub.start(i)
                v.wait_ge(blk_back, 16 * i + 16)
                sub.link(nc.vector.memset(YB, 0.0))
                sub.link(nc.vector.memset(strided(YB, (256, 2), (BK + 1, BK)), 1.0))
                for r in range(BK - 2, -1, -1):
                    m = BK - 1 - r
                    at = r * BK + r + 1
                    back = 256 + m * BK
                    coef = strided(BLK[:, at:at + 1], (back - at, 2), (1, m), (0, m))
                    below = (r + 1) * BK + r + 1
                    rows_done = strided(YB[:, below:below + 1], (256 - below, 2), (BK, m), (1, m))
                    prod = strided(PROD[:, 0:1], (256, 2), (BK, m), (1, m))
                    sub.link(nc.vector.tensor_tensor(prod, coef, rows_done, ALU.mult))
                    by_column = strided(PROD[:, 0:1], (256, 2), (1, m), (BK, m))
                    ins = nc.vector.tensor_reduce(strided(YB[:, at:at + 1], (back - at, 2), (1, m)), by_column, AX_X,
                                                  ALU.add, negate=True)
                    if r:
                        sub.link(ins)
                ins.then_inc(inv16_ready, 1)
                v.wait_ge(inv16_ready, 2 * i + 1)
                yb = YB.rearrange("q (e s t) -> q e s t", e=2, s=BK)
                nc.vector.tensor_copy(XB.rearrange("q (e s t) -> q e s t", e=2, s=BK), yb.rearrange("q e s t -> q e t s"))\
                  .then_inc(inv16_ready, 1)

            def doubling(i):
                banks = lambda b: PS[:, b:b + 2, 0:HALF].rearrange("p b (x t) -> p b x t", t=TC)
                split = lambda x: x.rearrange("p (b x) t -> p b x t", b=2)
                for l, wb, xb, yb in ((0, (0, 2), (4, 0), (6, 2)), (1, (4, 0), None, (6, 2))):
                    for e in range(2):
                        v.wait_ge(inv_w, 4 * i + 2 * l + e + 1)
                        m = LV[:, l, e:e + 1, :].unsqueeze(1).broadcast_to([128, 2, 6, TC])
                        nc.vector.tensor_tensor(split(WI[e][:, :, :]), banks(wb[e]), m, ALU.mult).then_inc(w_ready, 1)
                    for e in range(2):
                        v.wait_ge(inv_xy, 4 * i + 2 * l + e + 1)
                        if xb:
                            xs = split(XY[:, e])
                            nc.vector.tensor_tensor(xs, xs, banks(xb[e]), ALU.subtract)
                        ys = split(XY[:, 2 + e])
                        nc.vector.tensor_tensor(ys, ys, banks(yb[e]), ALU.subtract).then_inc(xy_ready, 1)

            def states(i):
                for n in range(NCH):
                    for e in range(2):
                        ch = order(e)[n]
                        pr = slice(64 * (ch % 2), 64 * (ch % 2) + 64)
                        j = ch // 2
                        v.wait_ge(rh_mm, 24 * i + 2 * n + e + 1)
                        if n == 0:
                            v.wait_ge(bv_ready, 2 * i + 2)
                        nc.vector.tensor_tensor(RHS[pr, :].rearrange("p (h t) -> p h t", h=2),
                                                BV[e][pr, 2 * j:2 * j + 2, :], PS[pr, 0:2, 0:64], ALU.add)\
                          .then_inc(rh_ready, 1)
                    for e in range(2):
                        ch = order(e)[n]
                        v.wait_ge(st_mm, 24 * i + 2 * n + e + 1)
                        v.wait_ge(st_ready[e], 13 * i + n + 1)
                        chain.link(nc.vector.tensor_tensor(STATE[:, e, :], STATE[:, e, :], PS[:, 3 + e, 0:64], ALU.add))
                        nc.vector.tensor_scalar(STATE[:, e, :], STATE[:, e, :], ENDS[:, e, ch:ch + 1], None, ALU.mult)\
                          .then_inc(st_ready[e], 1)

            with v.Fori(0, CT) as i:
                chain.start(i)
                vdyn = P[:, bass.ds(8 + i, 1), 0:L].rearrange("p a t -> p (a t)")
                features(0, i)
                masked(0, i)
                features(1, i)
                masked(1, i)
                substitution(i)
                doubling(i)
                states(i)
                v.wait_ge(y_mm, i + 1)
                chain.link(nc.vector.tensor_scalar(YS, PS[:, 5, :], 1.0, None, ALU.mult))
                for par in range(2):
                    of = lambda x: x.rearrange("p (j w t) -> p j w t", w=2, t=TC)[:, :, par, :]
                    last = nc.vector.tensor_tensor(of(YS), of(YS), of(PS[:, 6 + par, :]), ALU.add)
                last.then_inc(y_out, 1)
                v.wait_ge(mean_mm, i + 1)
                nc.vector.scalar_tensor_tensor(YS, PS[:, 0, :], -1.0 / CH, YS, ALU.mult, ALU.add).then_inc(centred, 1)
                v.wait_ge(cg_mm, i + 1)
                chain.link(nc.vector.tensor_tensor(EN[:, 0:L], PS[:, 2, :], vdyn, ALU.mult))
                v.wait_ge(gn_root, i + 1)
                chain.link(nc.vector.reciprocal(FIN, FIN))
                chain.link(nc.vector.tensor_tensor(YS, YS, FIN, ALU.mult))
                chain.link(nc.vector.tensor_scalar(YS, YS, PCS[:, PLW:PLW + 1], PCS[:, PLB:PLB + 1], ALU.mult, ALU.add))
                chain.link(nc.vector.tensor_tensor(YS, YS, EN[:, 0:L], ALU.add))
                nc.vector.tensor_tensor(Z[:, bass.ds(i, 1), :].rearrange("p a t -> p (a t)"), YS, PS[:, 3, :], ALU.mult)\
                  .then_inc(z_out, 1)
                chain.end()
                sub.end()
        mixout = Dense("mixout", "plain", 2, 30, a["rw_w_o"][0], lambda k: Z[:, k, :], H, L)
        gate1 = Dense("gate1", "gate", 11, 32, (a["ffn_w1"][1], a["ffn_w3"][1]), lambda k: Y[:, k, 0:L], P, L)
        down1 = Dense("down1", "long", 4, 43, a["ffn_w2"][1], lambda k: P[:, k, 0:L], H, L)
        Yt = lambda t: Y[:, t, :]
        Xt = lambda t: X[:, t, :]
        Xl = lambda t: X[:, t, 0:L]
        Hl = lambda t: H[:, t, 0:L]

        block = ctx.enter_context(nc.Block())

        @block.sync
        def _(sp):
            inputs_sp(sp)
            dense_load(sp, inproj, first=True)
            sp.wait_ge(x_evicted, 8)
            for dst, src in ((RPL[0:NH * ND, :], a["na_rpb"].rearrange("a h d m -> (a h d) m")),
                             (PICK[0:64, :], a["pick"]), (WINDOW, a["window"])):
                sp.dma_start(dst, src).then_inc(bias_in, 16)
            hyena_sp(sp)
            dense_load(sp, outproj)
            dense_load(sp, gate0)
            dense_load(sp, down0)
            mixes_sp(sp)
            dense_load(sp, value)
            dense_load(sp, key)
            dense_load(sp, recept)
            scan_sp(sp)
            sp.wait_ge(z_out, CT + 1)
            dense_load(sp, mixout)
            dense_load(sp, gate1)
            dense_load(sp, down1)
            output_sp(sp)

        @block.tensor
        def _(pe):
            inputs_pe(pe)
            norm_pe(pe, 0, T, lambda e: None)
            pe.wait_ge(normed, 8)
            dense_pe(pe, inproj)
            bias_pe(pe)
            attn_pe(pe)
            mlp_pe(pe)
            pe.wait_ge(attn_out, 2 + NH)
            pe.wait_ge(conv3_done, 12)
            hyena_pe(pe)
            pe.wait_ge(z_done, 16)
            dense_pe(pe, outproj)
            norm_pe(pe, 1, T, lambda e: None)
            norm_pe(pe, 2, T, lambda e: None)
            pe.wait_ge(normed, 16)
            dense_pe(pe, gate0)
            pe.wait_ge(gate0.unit_free, gate0.done)
            dense_pe(pe, down0)
            norm_pe(pe, 3, T, lambda e: None)
            norm_pe(pe, 4, T, lambda e: None)
            mixes_pe(pe)
            pe.wait_ge(lora_hid, 4)
            pe.wait_ge(mix_ready, 32)
            dense_pe(pe, value)
            pe.wait_ge(mix_ready, 40)
            pe.wait_ge(value.unit_free, value.done)
            dense_pe(pe, key)
            pe.wait_ge(mix_ready, 48)
            pe.wait_ge(key.unit_free, key.done)
            dense_pe(pe, recept)
            pe.wait_ge(recept.unit_free, recept.done)
            pe.wait_ge(scan_in, 64)
            pe.wait_ge(gate_hid, 2)
            scan_pe(pe)
            pe.wait_ge(z_out, CT + 1)
            dense_pe(pe, mixout)
            norm_pe(pe, 5, L, lambda e: None)
            norm_pe(pe, 6, L, lambda e: None)
            pe.wait_ge(normed, 32)
            dense_pe(pe, gate1)
            pe.wait_ge(gate1.unit_free, gate1.done)
            dense_pe(pe, down1)
            norm_pe(pe, 7, L, lambda e: None)
            output_pe(pe, 32)

        @block.scalar
        def _(act):
            inputs_act(act)
            act.wait_ge(consts_set, 3)
            norm_squares_act(act, 0, lambda t: X[:, t, :], T, lambda e, t: e.wait_ge(x_evicted, t + 1))
            act.wait_ge(gains_ready, 1)
            norm_shift_act(act, 0, T, 0, 0, Hf)
            dense_evict_act(act, inproj)
            attn_act(act)
            mlp_act(act)
            hyena_act(act)
            dense_evict_act(act, outproj)
            norm_squares_act(act, 1, lambda t: Y[:, t, :], T, lambda e, t: e.wait_ge(outproj.unit_free, outproj.done))
            norm_squares_act(act, 2, lambda t: X[:, t, :], T, lambda e, t: e.wait_ge(x_updated, t + 1))
            norm_shift_act(act, 2, T, 0, 2, Hf)
            dense_evict_act(act, gate0)
            dense_evict_act(act, down0)
            norm_squares_act(act, 3, lambda t: Y[:, t, :], T, lambda e, t: e.wait_ge(down0.unit_free, down0.done))
            norm_squares_act(act, 4, Xt, T, lambda e, t: e.wait_ge(x_updated, 8 + t + 1))
            norm_shift_act(act, 4, T, 1, 0, padded)
            mixes_act(act)
            dense_evict_act(act, value)
            dense_evict_act(act, key)
            dense_evict_act(act, recept)
            scan_act(act)
            dense_evict_act(act, mixout)
            norm_squares_act(act, 5, Hl, L, lambda e, t: e.wait_ge(mixout.unit_free, mixout.done))
            norm_squares_act(act, 6, Xl, L, lambda e, t: e.wait_ge(x_updated, 16 + t + 1))
            norm_shift_act(act, 6, L, 1, 2, lambda t, s0, s1: Y[:, t, s0:s1])
            dense_evict_act(act, gate1)
            dense_evict_act(act, down1)
            norm_squares_act(act, 7, Hl, L, lambda e, t: e.wait_ge(down1.unit_free, down1.done))
            output_act(act)

        @block.gpsimd
        def _(pool):
            attn_pool(pool)
            pool.wait_ge(slots_used, 4 * down0.base)
            for at in (0, L + 1, T + 2):
                nc.gpsimd.memset(Hpad[:, :, at:at + 1], 0.0).then_inc(pads_set, 1)
            scan_pool(pool)

        @block.vector
        def _(v):
            chain = Chain(v, dve_step)
            inputs_dve(v)
            v.wait_ge(gains_ready, 1)
            v.wait_ge(x_evicted, 8)
            norm_scale_dve(v, 0, lambda t: X[:, t, :], T)
            bias_dve(v)
            attn_dve(v)
            conv3_dve(v)
            mlp_dve(v, chain)
            hyena_dve(v, chain)
            norm_scale_dve(v, 1, lambda t: Y[:, t, :], T, residual=(0, 1))
            norm_scale_dve(v, 2, lambda t: X[:, t, :], T)
            gate_evict_dve(v, gate0, 0)
            norm_scale_dve(v, 3, Yt, T, residual=(0, 3))
            norm_scale_dve(v, 4, Xt, T)
            mixes_dve(v)
            scan_dve(v)
            v.wait_ge(x_back, 16)
            norm_scale_dve(v, 5, Hl, L, residual=(1, 1))
            norm_scale_dve(v, 6, Xl, L)
            gate_evict_dve(v, gate1, 22)
            norm_scale_dve(v, 7, Hl, L, residual=(1, 3))


_INS = ["x", "c", "ctx", "c_ctx", "mod_w", "mod_b", "norm_g", "ffn_w1", "ffn_w3", "ffn_w2", "mix_w_in", "mix_w_out",
        "na_rpb", "hy_short_w", "hy_short_b", "hy_pos_w1", "hy_pos_b1", "hy_pos_w2", "hy_pos_b2", "hy_pos_w3",
        "hy_sin_freq", "hy_skip", "rw_mu", "rw_w_rkv", "rw_w_o", "rw_w0", "rw_w1", "rw_w2", "rw_a0", "rw_a1",
        "rw_a2", "rw_g1", "rw_g2", "rw_k_k", "rw_k_a", "rw_r_k", "rw_ln_w", "rw_ln_b"]


def kernel(**inputs):
    import numpy as _np
    import concourse.bacc as _bacc
    from concourse import mybir as _mybir
    from concourse.bass_utils import run_bass_kernel_spmd as _run

    nc = _bacc.Bacc("TRN2", target_bir_lowering=False, num_devices=1)
    given = {name: _np.ascontiguousarray(inputs[name]) for name in _INS}
    given.update(shape_constants())
    arrays, aps = {}, {}
    for name, x in given.items():
        arrays[f"in_{name}_dram"] = x
        aps[name] = nc.dram_tensor(f"in_{name}_dram", x.shape, _mybir.dt.from_np(x.dtype), kind="ExternalInput").ap()
    out = nc.dram_tensor("out_0_dram", (1, L, D), F32, kind="ExternalOutput").ap()
    hybrid_dit_kernel(nc, aps, out)
    r = _run(nc, [arrays], core_ids=[0])
    return r.results[0]["out_0_dram"]
```
